# Optimizing a Trainium2 kernel written in Bass

```python
import jax, jax.numpy as jnp
from jax import lax
import numpy as np
import math

D_MODEL = 1024
BATCH = 1
SEQ = 256
DEPTH = 1

MIX_WIDTH = D_MODEL
POOL_WIDTH = MIX_WIDTH // 2
POOL_WINDOWS = (2, 4, 8, 16)
N_POOL_GROUPS = len(POOL_WINDOWS)
POOL_GROUP_DIM = POOL_WIDTH // N_POOL_GROUPS
RET_WIDTH = MIX_WIDTH - POOL_WIDTH
RET_HEADS = 4
RET_HEAD_DIM = RET_WIDTH // RET_HEADS
RET_CHUNK = 128
ROPE_BASE = 10000.0
IN_WIDTH = POOL_WIDTH + 4 * RET_WIDTH
D_FF = 2816
EPS = 1e-6


def rmsnorm(x, gain):
    xf = x.astype(jnp.float32)
    y = xf * lax.rsqrt(jnp.mean(xf * xf, axis=-1, keepdims=True) + EPS)
    return (y * gain.astype(jnp.float32)).astype(x.dtype)

def swiglu(x, w1, w3, w2):
    return (jax.nn.silu(x @ w1) * (x @ w3)) @ w2

def pool_mixer(u, pool_w, pool_scale):
    B, S, _ = u.shape
    ug = u.reshape(B, S, N_POOL_GROUPS, POOL_GROUP_DIM)
    t = jnp.arange(1, S + 1, dtype=jnp.float32)
    outs = []
    for gi, w in enumerate(POOL_WINDOWS):
        xg = ug[:, :, gi, :]
        cs = lax.cumsum(xg.astype(jnp.float32), axis=1)
        csp = jnp.pad(cs, ((0, 0), (w, 0), (0, 0)))
        window_sum = csp[:, w:, :] - csp[:, :S, :]
        count = jnp.minimum(t, float(w))[None, :, None]
        pooled = (window_sum / count).astype(u.dtype) - xg
        outs.append(pooled @ pool_w[gi])
    return jnp.concatenate(outs, axis=-1) * pool_scale

def rope_tables(S, D):
    inv_freq = 1.0 / (ROPE_BASE ** (jnp.arange(0, D, 2, dtype=jnp.float32) / D))
    ang = jnp.arange(S, dtype=jnp.float32)[:, None] * inv_freq[None, :]
    return jnp.cos(ang), jnp.sin(ang)

def apply_rope(t, cos, sin):
    t1, t2 = jnp.split(t, 2, axis=-1)
    c = cos[None, :, None, :]
    s = sin[None, :, None, :]
    return jnp.concatenate([t1 * c - t2 * s, t1 * s + t2 * c], axis=-1)

def retention(q, k, v, g, gain):
    B, S, _ = q.shape
    H, D, C = RET_HEADS, RET_HEAD_DIM, RET_CHUNK
    NC = S // C
    dt = q.dtype

    def heads(t):
        return t.astype(jnp.float32).reshape(B, S, H, D)

    cos, sin = rope_tables(S, D)
    qh = apply_rope(heads(q), cos, sin)
    kh = apply_rope(heads(k), cos, sin) * (D ** -0.5)
    vh = heads(v)

    def chunks(t):
        return t.reshape(B, NC, C, H, D).transpose(0, 3, 1, 2, 4)

    qc, kc, vc = chunks(qh), chunks(kh), chunks(vh)

    log_gamma = jnp.log1p(-jnp.exp2(-5.0 - jnp.arange(H, dtype=jnp.float32)))
    pos = jnp.arange(C, dtype=jnp.float32)
    rel = pos[:, None] - pos[None, :]
    intra_decay = jnp.where(rel[None] >= 0,
                            jnp.exp(log_gamma[:, None, None] * jnp.maximum(rel, 0.0)[None]),
                            0.0)

    scores = jnp.einsum('bhncd,bhnsd->bhncs', qc, kc) * intra_decay[None, :, None]
    o_intra = jnp.einsum('bhncs,bhnse->bhnce', scores, vc)

    k_tail = jnp.exp(log_gamma[:, None] * (C - 1 - pos)[None, :])
    kv = jnp.einsum('bhnsd,bhnse->nbhde', kc * k_tail[None, :, None, :, None], vc)
    chunk_decay = jnp.exp(log_gamma * C)[None, :, None, None]

    def step(R, kv_n):
        return chunk_decay * R + kv_n, R

    _, R_prev = lax.scan(step, jnp.zeros((B, H, D, D), jnp.float32), kv)

    q_head = jnp.exp(log_gamma[:, None] * (pos + 1.0)[None, :])
    o_cross = jnp.einsum('bhncd,nbhde->bhnce', qc * q_head[None, :, None, :, None], R_prev)

    o = (o_intra + o_cross).transpose(0, 2, 3, 1, 4).reshape(B, S, H, D)
    o = o * lax.rsqrt(jnp.mean(o * o, axis=-1, keepdims=True) + EPS)
    o = o.reshape(B, S, H * D) * gain.astype(jnp.float32)
    return (jax.nn.silu(g.astype(jnp.float32)) * o).astype(dt)

def first_inputs(seed: int = 0) -> dict:
    key = jax.random.key(seed)
    ks = jax.random.split(key, 20)
    f32 = jnp.float32

    def nrm(k, shape, fan_in):
        return jax.random.normal(k, shape, f32) * (fan_in ** -0.5)

    def gain(k, shape):
        return 1.0 + 0.05 * jax.random.normal(k, shape, f32)

    L = DEPTH
    return {
        "x": jax.random.normal(ks[0], (BATCH, SEQ, D_MODEL), f32),
        "ffn1_norm": gain(ks[1], (L, D_MODEL)),
        "ffn1_w1": nrm(ks[2], (L, D_MODEL, D_FF), D_MODEL),
        "ffn1_w3": nrm(ks[3], (L, D_MODEL, D_FF), D_MODEL),
        "ffn1_w2": nrm(ks[4], (L, D_FF, D_MODEL), D_FF),
        "mix_norm": gain(ks[5], (L, D_MODEL)),
        "w_in": nrm(ks[6], (L, D_MODEL, IN_WIDTH), D_MODEL),
        "pool_w": nrm(ks[7], (L, N_POOL_GROUPS, POOL_GROUP_DIM, POOL_GROUP_DIM), POOL_GROUP_DIM),
        "pool_scale": gain(ks[8], (L, POOL_WIDTH)),
        "ret_norm": gain(ks[9], (L, RET_WIDTH)),
        "w_out": nrm(ks[10], (L, MIX_WIDTH, D_MODEL), MIX_WIDTH),
        "ffn2_norm": gain(ks[11], (L, D_MODEL)),
        "ffn2_w1": nrm(ks[12], (L, D_MODEL, D_FF), D_MODEL),
        "ffn2_w3": nrm(ks[13], (L, D_MODEL, D_FF), D_MODEL),
        "ffn2_w2": nrm(ks[14], (L, D_FF, D_MODEL), D_FF),
        "final_norm": gain(ks[15], (D_MODEL,)),
    }

def first_block(x, ffn1_norm, ffn1_w1, ffn1_w3, ffn1_w2, mix_norm, w_in, pool_w, pool_scale,
              ret_norm, w_out, ffn2_norm, ffn2_w1, ffn2_w3, ffn2_w2, final_norm):
    h = x
    for l in range(DEPTH):
        h = h + 0.5 * swiglu(rmsnorm(h, ffn1_norm[l]), ffn1_w1[l], ffn1_w3[l], ffn1_w2[l])

        u = rmsnorm(h, mix_norm[l])
        proj = u @ w_in[l]
        u_pool, q, k, v, g = jnp.split(
            proj, [POOL_WIDTH, POOL_WIDTH + RET_WIDTH, POOL_WIDTH + 2 * RET_WIDTH,
                   POOL_WIDTH + 3 * RET_WIDTH], axis=-1)
        a = pool_mixer(u_pool, pool_w[l], pool_scale[l])
        b = retention(q, k, v, g, ret_norm[l])
        h = h + jnp.concatenate([a, b], axis=-1) @ w_out[l]

        h = h + 0.5 * swiglu(rmsnorm(h, ffn2_norm[l]), ffn2_w1[l], ffn2_w3[l], ffn2_w2[l])
    return rmsnorm(h, final_norm)


HEAD_DIM = 64
A_HEADS = 8
A_KV_HEADS = 2
A_WINDOW = 128
B_HEADS = 8
B_KV_GROUPS = 2
CMP_BLOCK = 32
CMP_STRIDE = 16
CMP_HIDDEN = 256
SLC_BLOCK = 64
SLC_TOPK = 16
NSA_WINDOW = 512
NUM_BUCKETS = 32
MAX_DISTANCE = 128
CONV_WIDTH = 3
Q_BLOCK = 128
NEG = -1e30
BIG = 1e30

A_Q_DIM = A_HEADS * HEAD_DIM
A_KV_DIM = A_KV_HEADS * HEAD_DIM
B_Q_DIM = B_HEADS * HEAD_DIM
B_KV_DIM = B_KV_GROUPS * HEAD_DIM
B_GATE_DIM = 3 * B_HEADS
IN_SPLITS = (A_Q_DIM, A_KV_DIM, A_KV_DIM, B_Q_DIM, B_KV_DIM, B_KV_DIM, B_KV_DIM, B_KV_DIM, B_KV_DIM, B_KV_DIM, B_GATE_DIM, D_MODEL, D_MODEL)
IN_DIM = sum(IN_SPLITS)
IN_OFFSETS = tuple(int(o) for o in np.cumsum(IN_SPLITS)[:-1])


def rmsnorm_2(x, g):
    xf = x.astype(jnp.float32)
    y = xf * lax.rsqrt(jnp.mean(xf * xf, axis=-1, keepdims=True) + EPS)
    return (y * g.astype(jnp.float32)).astype(x.dtype)

def t5_bucket(dist):
    dist = jnp.maximum(dist, 0)
    max_exact = NUM_BUCKETS // 2
    d = jnp.maximum(dist, 1).astype(jnp.float32)
    large = max_exact + (jnp.log(d / max_exact) / math.log(MAX_DISTANCE / max_exact)
                         * (NUM_BUCKETS - max_exact)).astype(jnp.int32)
    large = jnp.minimum(large, NUM_BUCKETS - 1)
    return jnp.where(dist < max_exact, dist, large)

def head_bias(table_gr, dist):
    return jnp.transpose(table_gr[t5_bucket(dist)], (2, 3, 0, 1))

def selection_overlap(n_cmp, n_slc):
    r = SLC_BLOCK // CMP_STRIDE
    c = CMP_BLOCK // CMP_STRIDE
    j, m, n = np.meshgrid(np.arange(n_slc), np.arange(r), np.arange(c), indexing='ij')
    i = r * j + m - n
    ok = (i >= 0) & (i < n_cmp)
    mat = np.zeros((n_cmp, n_slc), np.float32)
    np.add.at(mat, (i[ok], j[ok]), 1.0)
    return mat

def causal_dwconv(u, w, b):
    c = u.shape[-1]
    out = lax.conv_general_dilated(u, w[:, None, :].astype(u.dtype), window_strides=(1,),
                                   padding=[(CONV_WIDTH - 1, 0)],
                                   dimension_numbers=('NWC', 'WIO', 'NWC'),
                                   feature_group_count=c)
    return out + b

def swa_sink_attention(q, k, v, sinks, table):
    bsz, seq, n_heads, dh = q.shape
    n_groups = k.shape[2]
    rep = n_heads // n_groups
    span = A_WINDOW + Q_BLOCK
    qg = q.reshape(bsz, seq, n_groups, rep, dh)
    kp = jnp.pad(k, ((0, 0), (A_WINDOW, 0), (0, 0), (0, 0)))
    vp = jnp.pad(v, ((0, 0), (A_WINDOW, 0), (0, 0), (0, 0)))
    qi = jnp.arange(Q_BLOCK)[:, None]
    ki = jnp.arange(span)[None, :]
    dist = qi + A_WINDOW - ki
    in_window = (dist >= 0) & (dist < A_WINDOW)
    bias = head_bias(table.reshape(NUM_BUCKETS, n_groups, rep), dist)
    sink = sinks.astype(jnp.float32).reshape(n_groups, rep)
    scale = dh ** -0.5

    def block(b):
        start = b * Q_BLOCK
        qb = lax.dynamic_slice_in_dim(qg, start, Q_BLOCK, axis=1)
        kb = lax.dynamic_slice_in_dim(kp, start, span, axis=1)
        vb = lax.dynamic_slice_in_dim(vp, start, span, axis=1)
        valid = in_window & (start - A_WINDOW + ki >= 0)
        logits = jnp.einsum('bqgrd,bkgd->bgrqk', qb, kb, preferred_element_type=jnp.float32) * scale + bias
        logits = jnp.where(valid, logits, NEG)
        sink_col = jnp.broadcast_to(sink[None, :, :, None, None], logits.shape[:-1] + (1,))
        probs = jax.nn.softmax(jnp.concatenate([logits, sink_col], axis=-1), axis=-1)[..., :span]
        out = jnp.einsum('bgrqk,bkgd->bqgrd', probs.astype(v.dtype), vb)
        return out.reshape(bsz, Q_BLOCK, n_heads * dh)

    out = lax.map(block, jnp.arange(seq // Q_BLOCK))
    return jnp.transpose(out, (1, 0, 2, 3)).reshape(bsz, seq, n_heads * dh)

def compress(kv, pos, w1, w2):
    bsz, seq, n_groups, dh = kv.shape
    n_cmp = (seq - CMP_BLOCK) // CMP_STRIDE + 1
    idx = jnp.arange(n_cmp)[:, None] * CMP_STRIDE + jnp.arange(CMP_BLOCK)[None, :]
    blocks = kv[:, idx] + pos[None, None, :, None, :]
    blocks = jnp.transpose(blocks, (0, 1, 3, 2, 4)).reshape(bsz, n_cmp, n_groups, CMP_BLOCK * dh)
    return jax.nn.gelu(blocks @ w1) @ w2

def nsa_attention(q, k_cmp, v_cmp, k_slc, v_slc, k_win, v_win, gates, table):
    bsz, seq, n_heads, dh = q.shape
    n_groups = k_slc.shape[2]
    rep = n_heads // n_groups
    n_cmp = k_cmp.shape[1]
    n_slc = seq // SLC_BLOCK
    topk = min(SLC_TOPK, n_slc)
    n_tok = topk * SLC_BLOCK
    scale = dh ** -0.5
    qg = q.reshape(bsz, seq, n_groups, rep, dh)
    table_gr = table.reshape(NUM_BUCKETS, n_groups, rep)
    table_g = jnp.transpose(table_gr, (1, 0, 2))
    cmp_end = jnp.arange(n_cmp) * CMP_STRIDE + CMP_BLOCK - 1
    overlap = jnp.asarray(selection_overlap(n_cmp, n_slc))
    k_slc_g = jnp.transpose(k_slc, (0, 2, 1, 3))
    v_slc_g = jnp.transpose(v_slc, (0, 2, 1, 3))
    span = NSA_WINDOW + Q_BLOCK
    kwp = jnp.pad(k_win, ((0, 0), (NSA_WINDOW, 0), (0, 0), (0, 0)))
    vwp = jnp.pad(v_win, ((0, 0), (NSA_WINDOW, 0), (0, 0), (0, 0)))
    qi = jnp.arange(Q_BLOCK)[:, None]
    ki = jnp.arange(span)[None, :]
    dist_w = qi + NSA_WINDOW - ki
    in_window = (dist_w >= 0) & (dist_w < NSA_WINDOW)
    bias_w = head_bias(table_gr, dist_w)
    bidx = jnp.arange(bsz)[:, None, None, None]
    gidx = jnp.arange(n_groups)[None, :, None, None]
    slc_ids = jnp.arange(n_slc)[None, :]

    def block(b):
        start = b * Q_BLOCK
        qpos = start + jnp.arange(Q_BLOCK)
        qb = lax.dynamic_slice_in_dim(qg, start, Q_BLOCK, axis=1)
        dist_c = qpos[:, None] - cmp_end[None, :]
        valid_c = dist_c >= 0
        lc = jnp.einsum('bqgrd,bcgd->bgrqc', qb, k_cmp, preferred_element_type=jnp.float32) * scale
        lc = jnp.where(valid_c, lc + head_bias(table_gr, dist_c), NEG)
        p_c = jax.nn.softmax(lc, axis=-1) * valid_c
        o_c = jnp.einsum('bgrqc,bcgd->bqgrd', p_c.astype(v_cmp.dtype), v_cmp)
        imp = jnp.einsum('bgrqc,cj->bgqj', p_c, overlap)
        qblk = (qpos // SLC_BLOCK)[:, None]
        forced = (slc_ids == 0) | (slc_ids == qblk) | (slc_ids == qblk - 1)
        score = jnp.where(forced, BIG, jnp.where(slc_ids > qblk, NEG, imp))
        _, sel = lax.top_k(score, topk)
        tok = (sel[..., None] * SLC_BLOCK + jnp.arange(SLC_BLOCK)).reshape(bsz, n_groups, Q_BLOCK, n_tok)
        ks = k_slc_g[bidx, gidx, tok]
        vs = v_slc_g[bidx, gidx, tok]
        dist_s = qpos[None, None, :, None] - tok
        bias_s = jnp.transpose(table_g[gidx, t5_bucket(dist_s)], (0, 1, 4, 2, 3))
        ls = jnp.einsum('bqgrd,bgqtd->bgrqt', qb, ks, preferred_element_type=jnp.float32) * scale + bias_s
        ls = jnp.where((dist_s >= 0)[:, :, None], ls, NEG)
        p_s = jax.nn.softmax(ls, axis=-1)
        o_s = jnp.einsum('bgrqt,bgqtd->bqgrd', p_s.astype(v_slc.dtype), vs)
        kb = lax.dynamic_slice_in_dim(kwp, start, span, axis=1)
        vb = lax.dynamic_slice_in_dim(vwp, start, span, axis=1)
        valid_w = in_window & (start - NSA_WINDOW + ki >= 0)
        lw = jnp.einsum('bqgrd,bkgd->bgrqk', qb, kb, preferred_element_type=jnp.float32) * scale + bias_w
        p_w = jax.nn.softmax(jnp.where(valid_w, lw, NEG), axis=-1)
        o_w = jnp.einsum('bgrqk,bkgd->bqgrd', p_w.astype(v_win.dtype), vb)
        gb = lax.dynamic_slice_in_dim(gates, start, Q_BLOCK, axis=1)
        out = gb[..., 0:1] * o_c + gb[..., 1:2] * o_s + gb[..., 2:3] * o_w
        return out.reshape(bsz, Q_BLOCK, n_heads * dh)

    out = lax.map(block, jnp.arange(seq // Q_BLOCK))
    return jnp.transpose(out, (1, 0, 2, 3)).reshape(bsz, seq, n_heads * dh)

def second_inputs(seed: int = 0) -> dict:
    key = jax.random.key(seed)
    ks = jax.random.split(key, 20)
    f32 = jnp.float32

    def nrm(k, shape, scale):
        return jax.random.normal(k, shape, f32) * scale

    L, D = DEPTH, D_MODEL
    cmp_in = CMP_BLOCK * HEAD_DIM
    return {
        'x': nrm(ks[0], (BATCH, SEQ, D), 1.0),
        'norm_mix': 1.0 + nrm(ks[1], (L, D), 0.02),
        'w_in': nrm(ks[2], (L, D, IN_DIM), D ** -0.5),
        'attn_sinks': nrm(ks[3], (L, A_HEADS), 0.5),
        'cmp_pos_k': nrm(ks[4], (L, CMP_BLOCK, HEAD_DIM), 0.1),
        'cmp_w1_k': nrm(ks[5], (L, cmp_in, CMP_HIDDEN), cmp_in ** -0.5),
        'cmp_w2_k': nrm(ks[6], (L, CMP_HIDDEN, HEAD_DIM), CMP_HIDDEN ** -0.5),
        'cmp_pos_v': nrm(ks[7], (L, CMP_BLOCK, HEAD_DIM), 0.1),
        'cmp_w1_v': nrm(ks[8], (L, cmp_in, CMP_HIDDEN), cmp_in ** -0.5),
        'cmp_w2_v': nrm(ks[9], (L, CMP_HIDDEN, HEAD_DIM), CMP_HIDDEN ** -0.5),
        'w_up_a': nrm(ks[10], (L, A_Q_DIM, D), A_Q_DIM ** -0.5),
        'w_up_b': nrm(ks[11], (L, B_Q_DIM, D), B_Q_DIM ** -0.5),
        'w_out': nrm(ks[12], (L, D, D), D ** -0.5),
        'norm_ffn': 1.0 + nrm(ks[13], (L, D), 0.02),
        'w_ffn_in': nrm(ks[14], (L, D, 2 * D_FF), D ** -0.5),
        'conv_w': nrm(ks[15], (L, CONV_WIDTH, 2 * D_FF), CONV_WIDTH ** -0.5),
        'conv_b': nrm(ks[16], (L, 2 * D_FF), 0.01),
        'w_ffn_out': nrm(ks[17], (L, D_FF, D), D_FF ** -0.5),
        'rel_bias_table': nrm(ks[18], (NUM_BUCKETS, A_HEADS + B_HEADS), 0.5),
        'norm_final': 1.0 + nrm(ks[19], (D,), 0.02),
    }

def second_block(x, norm_mix, w_in, attn_sinks, cmp_pos_k, cmp_w1_k, cmp_w2_k, cmp_pos_v, cmp_w1_v, cmp_w2_v,
              w_up_a, w_up_b, w_out, norm_ffn, w_ffn_in, conv_w, conv_b, w_ffn_out, rel_bias_table, norm_final):
    bsz, seq, _ = x.shape
    table_a = rel_bias_table[:, :A_HEADS]
    table_b = rel_bias_table[:, A_HEADS:]

    def heads(t, n):
        return t.reshape(bsz, seq, n, HEAD_DIM)

    for l in range(DEPTH):
        h = rmsnorm_2(x, norm_mix[l])
        proj = h @ w_in[l]
        (qa, ka, va, qb, kc, vc, ksl, vsl, kw, vw, g_nsa, g_a, g_b) = jnp.split(proj, IN_OFFSETS, axis=-1)
        y_a = swa_sink_attention(heads(qa, A_HEADS), heads(ka, A_KV_HEADS), heads(va, A_KV_HEADS),
                                 attn_sinks[l], table_a)
        k_cmp = compress(heads(kc, B_KV_GROUPS), cmp_pos_k[l], cmp_w1_k[l], cmp_w2_k[l])
        v_cmp = compress(heads(vc, B_KV_GROUPS), cmp_pos_v[l], cmp_w1_v[l], cmp_w2_v[l])
        nsa_gates = jax.nn.sigmoid(g_nsa).reshape(bsz, seq, B_KV_GROUPS, B_HEADS // B_KV_GROUPS, 3)
        y_b = nsa_attention(heads(qb, B_HEADS), k_cmp, v_cmp, heads(ksl, B_KV_GROUPS), heads(vsl, B_KV_GROUPS),
                            heads(kw, B_KV_GROUPS), heads(vw, B_KV_GROUPS), nsa_gates, table_b)
        merged = jax.nn.sigmoid(g_a) * (y_a @ w_up_a[l]) + jax.nn.sigmoid(g_b) * (y_b @ w_up_b[l])
        x = x + merged @ w_out[l]
        h = rmsnorm_2(x, norm_ffn[l])
        ug = causal_dwconv(h @ w_ffn_in[l], conv_w[l], conv_b[l])
        u, g = jnp.split(ug, 2, axis=-1)
        x = x + (jax.nn.silu(g) * u) @ w_ffn_out[l]
    return rmsnorm_2(x, norm_final)


def setup_inputs(seed=0):
    out = dict(first_inputs(seed))
    for name, value in second_inputs(seed + 1).items():
        if name != "x":
            out[name + "_2"] = value
    return out


def reference(
    x, ffn1_norm, ffn1_w1, ffn1_w3, ffn1_w2, mix_norm, w_in, pool_w, pool_scale, ret_norm,
    w_out, ffn2_norm, ffn2_w1, ffn2_w3, ffn2_w2, final_norm, norm_mix_2, w_in_2, attn_sinks_2,
    cmp_pos_k_2, cmp_w1_k_2, cmp_w2_k_2, cmp_pos_v_2, cmp_w1_v_2, cmp_w2_v_2, w_up_a_2,
    w_up_b_2, w_out_2, norm_ffn_2, w_ffn_in_2, conv_w_2, conv_b_2, w_ffn_out_2,
    rel_bias_table_2, norm_final_2,
):
    x = first_block(
        x, ffn1_norm, ffn1_w1, ffn1_w3, ffn1_w2, mix_norm, w_in, pool_w, pool_scale, ret_norm,
        w_out, ffn2_norm, ffn2_w1, ffn2_w3, ffn2_w2, final_norm,
    )
    return second_block(
        x, norm_mix_2, w_in_2, attn_sinks_2, cmp_pos_k_2, cmp_w1_k_2, cmp_w2_k_2, cmp_pos_v_2,
        cmp_w1_v_2, cmp_w2_v_2, w_up_a_2, w_up_b_2, w_out_2, norm_ffn_2, w_ffn_in_2, conv_w_2,
        conv_b_2, w_ffn_out_2, rel_bias_table_2, norm_final_2,
    )


_drawn_inputs = setup_inputs


def setup_inputs(seed=0):
    import zlib

    import numpy as np

    out = dict(_drawn_inputs(seed))
    spreads = {}
    factors = {'ret_norm': 2.996,
     'ffn2_norm': 3.01,
     'norm_mix_2': 8.0,
     'attn_sinks_2': 8.0,
     'cmp_pos_k_2': 8.0,
     'cmp_pos_v_2': 11.952,
     'norm_ffn_2': 3.833,
     'conv_b_2': 7.981}
    for name, (base, spread) in spreads.items():
        noise = np.random.default_rng([zlib.crc32(name.encode()), seed]).standard_normal(out[name].shape)
        drawn = base * np.exp(spread * noise) if base else spread * noise
        out[name] = __import__('jax').numpy.asarray(drawn.astype(out[name].dtype))
    for name, factor in factors.items():
        out[name] = (out[name] * factor).astype(out[name].dtype)
    return out
```

```python
from contextlib import ExitStack

import concourse.bass as bass
from concourse import mybir

F32 = mybir.dt.float32
F32R = mybir.dt.float32r
BF16 = mybir.dt.bfloat16
I32 = mybir.dt.int32
ALU = mybir.AluOpType
ACT = mybir.ActivationFunctionType
AX_X = mybir.AxisListType.X

P = 128
T = 256
D = 1024
DC = D // P
FF = 2816
EPS = 1e-6
SLOTS = 3
UNIT = 2048
UC = UNIT // DC
FI = FF // UC
NEG = -1e30

HR = 4
POOL_WINDOWS = (2, 4, 8, 16)
PAD = 16
DEC = T + P

HD = 64
NHA = 8
NCMP = 15
NBUCKET = 32
BIASW = 384

OH_D0, OH_COLS = 256, 640
BIAS_D0 = P - 1
NBR = 3
SLOTS_A = 18
GA, GB, CW = (8, 9, 10, 11), (12, 13, 18, 19), (14, 15, 16, 17)

U_FFN1 = 0
U_MIX = U_FFN1 + 3 * FI
U_OUT1 = U_MIX + 10
U_FFN2 = U_OUT1 + 4
U_IN2 = U_FFN2 + 3 * FI
U_UP = U_IN2 + 20
U_OUT2 = U_UP + 4
U_FFN3 = U_OUT2 + 4


def slot_time(s):
    return s if s < 6 else s + 2


def position_time(m, half):
    pos = 2 * m + half
    if 8 <= pos < 16:
        return pos - 8
    return pos - 10 if 18 <= pos < 32 else None


V_FFN1, V_MIX, V_FFN2, V_FINAL, V_MIX2, V_FFN3, V_FINAL2 = (8 * n for n in range(7))
V_POOL, V_RET, V_POSK, V_POSV, V_COLS = 56, 60, 64, 80, 96

C_ID, C_SWAP, C_NEGC, C_VALC, C_BLK, C_COLS = 0, 128, 256, 286, 316, 324
T_COS, T_SIN, T_DEC, T_RC, T_COLS = 0, 256, 512, 512 + HR * DEC, 512 + HR * DEC + 4 * T


def rows8(v):
    return v.rearrange("(c p) -> c p", p=P)


def bcast(ap, n):
    return ap.unsqueeze(1).to_broadcast([ap.shape[0], n, ap.shape[1]])


def bcast_in(ap, n):
    return ap.unsqueeze(2).to_broadcast([ap.shape[0], ap.shape[1], n])


def build(nc, a, out):
    with ExitStack() as ctx:
        def sb(name, shape, dt=F32):
            return ctx.enter_context(nc.sbuf_tensor(name, shape, dt))

        def sem(name):
            return ctx.enter_context(nc.semaphore(name))

        raw = sb("raw", [P, SLOTS, UNIT])
        w_hi = sb("w_hi", [P, SLOTS, UNIT], F32R)
        w_lo = sb("w_lo", [P, SLOTS, UNIT], F32R)
        x = sb("x", [P, DC, T])
        xh = sb("xh", [P, DC, T], F32R)
        xl = sb("xl", [P, DC, T], F32R)
        mh = sb("mh", [P, DC, T], F32R)
        ml = sb("ml", [P, DC, T], F32R)
        hh = sb("hh", [P, 2, T], F32R)
        hl = sb("hl", [P, 2, T], F32R)
        sq = sb("sq", [P, DC, T])
        work = sb("work", [P, 6, 2 * T])
        arena = sb("arena", [P, 63 * 256])
        cst = sb("cst", [P, C_COLS])
        ones = sb("ones", [P, P])
        mean_d = sb("mean_d", [P, 1])
        mean_h = sb("mean_h", [P, 1])
        zeros = sb("zeros", [P, 512], BF16)
        vec = sb("vec", [P, V_COLS])
        rstd_t = sb("rstd_t", [P, 2])
        rstd_b = sb("rstd_b", [P, T])
        nr = sb("nr", [P, 3, 8])

        a_s, b_s, t_s, h_s = (work[:, n] for n in range(4))
        diag = work[:, 5, 0:T].rearrange("p (t q) -> p t q", t=2)
        ident = cst[:, C_ID:C_ID + P]
        swap = cst[:, C_SWAP:C_SWAP + P]

        def carve(kib, *shape):
            n = 1
            for s in shape:
                n *= s
            lo = int(kib * 256)
            flat = arena[:, lo:lo + n]
            if len(shape) == 1:
                return flat
            names = " ".join("abcd"[:len(shape)])
            return flat.rearrange(f"p ({names}) -> p {names}", **dict(zip("abcd", shape)))

        x_tok = carve(0, 2, D)
        vec_rows = carve(8, P)

        q_s, k_s = carve(0, HR, T), carve(4, HR, T)
        diag_h = carve(0, 8, P)
        b_h = carve(4, HR, T)
        q_r, k_r = carve(8, HR, T), carve(12, HR, T)
        v_t = carve(16, 2, HR * P)
        pool_u = carve(20, 4, PAD + T)
        win_a, win_b = carve(24.25, 4, PAD + T), carve(28.5, 4, PAD + T)
        o_s = carve(28.5, HR, T)
        st = carve(20, HR, DEC)
        pooled = carve(32.75, 4, T)
        table = carve(36.75, T_COLS)
        pool_ws = carve(48.75, 4, P)
        g_s = work[:, 0:2]
        g_t = work[:, 2:4]
        o_sq = sq[:, 0:HR]

        acc = ctx.enter_context(nc.psum_tensor("acc", [P, 4, 512], F32))
        wk = ctx.enter_context(nc.psum_tensor("wk", [P, 4, 512], F32))

        oh = carve(51, OH_COLS)[0:NBUCKET]
        bias_mask = carve(54.5, BIASW)[0:16]
        bias_rows = carve(56, BIASW)[0:16]
        bias_table = carve(57.5, 16)[0:NBUCKET]
        conv_rows = carve(58, 4, P)[0:44]
        bias_c = carve(62, 2, NHA, NCMP)
        bias = carve(0, 16, T)
        ga, gb = carve(16, DC, T), carve(24, DC, T)
        blk = carve(24, 2, 16, 32)
        kz = [carve(32 + 4 * n, 2, 2, T) for n in range(2)]
        qa_s, qb_s = carve(40, 4, T), carve(44, 4, T)
        logit = [carve(48 + 2 * n, 512) for n in range(2)]
        prob = [carve(52 + 2 * n, 512) for n in range(2)]
        prob_t = [carve(56 + 2 * n, 512) for n in range(2)]
        v2 = [carve(60 + n, 2, P) for n in range(2)]
        v_blk = carve(48, 8, HD)
        prob_ct = carve(52, 2, P)
        sqf = sq[:].rearrange("p c t -> p (c t)")
        kf = sqf[:, 0:5 * T].rearrange("p (n t) -> p n t", n=5)
        K_A, K_S, K_W, K_CK, K_CV = range(5)
        cmp_w2 = sqf[:, 0:384].rearrange("p (n d) -> p n d", n=2)
        hv_rep = sqf[:, 2 * T:3 * T].rearrange("p (n m) -> p n m", n=2)
        prob_c = sqf[:, 1280:1536].rearrange("p (m c) -> p m c", c=16)
        hid_x, hid_z, hid_t = (sqf[:, 1536 + n * P:1536 + (n + 1) * P] for n in range(3))
        hid_k = sqf[:, 1920:1984].rearrange("p (n m) -> p n m", n=2)
        kcz = sqf[:, 1984:2048].rearrange("p (h m) -> p h m", h=2)
        y_a, y_b, y_tmp = work[:, 0:2], work[:, 2:4], work[:, 4]
        wg_raw = work[:, 5, T:T + 192].rearrange("p (k n) -> p k n", k=DC)
        wg_hi, wg_lo = sb("wg_hi", [P, DC, 24], F32R), sb("wg_lo", [P, DC, 24], F32R)
        conv = sb("conv", [P, 4, 44])
        sink = sb("sink", [P, NHA])
        gates = sb("gates", [P, 2, 24])
        half_r = sb("half_r", [P, 2])
        mx, nmx, sums = (sb(n, [P, NBR, 2, NHA]) for n in ("mx", "nmx", "sums"))
        coef = sb("coef", [P, 2, NHA])
        mx_c, sum_c = sb("mx_c", [P, 16]), sb("sum_c", [P, 16])
        blk_hl = [t[:, 4:8].rearrange("p a b -> p (a b)").rearrange("p (v j m) -> p v j m", v=2, j=16)
                  for t in (mh, ml)]
        conv_a, conv_b, t3_s, h3_s = (work[:, n] for n in range(2, 6))
        out_s = carve(0, 2, D)
        scratch = nc.dram_tensor("bias_scratch", (16, BIASW), F32, kind="Internal").ap()

        def acc_tile(n):
            return acc[:, n // 2, (n % 2) * T:(n % 2 + 1) * T]

        def halves(bank):
            return bank.rearrange("p (h t) -> p h t", t=T)

        raw_in = [sem(f"raw_in{s}") for s in range(SLOTS)]
        hi_done, lo_done, unit_done = sem("hi_done"), sem("lo_done"), sem("unit_done")
        first_in, table_in, pw_in = sem("first_in"), sem("table_in"), sem("pw_in")
        vec_zero = sem("vec_zero")
        const_set = sem("const_set")
        vec_turned, vec_ready = sem("vec_turned"), sem("vec_ready")
        acc_ready, x_ready, xh_ready, xl_ready, sq_ready = (
            sem(n) for n in ("acc_ready", "x_ready", "xh_ready", "xl_ready", "sq_ready"))
        ms_ready, diag_ready, spread_ready, rstd_ready = (
            sem(n) for n in ("ms_ready", "diag_ready", "spread_ready", "rstd_ready"))
        dve_step = sem("dve_step")
        a_out, tanh_out, b_out, h1_out, h_out, hh_out, hl_out = (
            sem(n) for n in ("a_out", "tanh_out", "b_out", "h1_out", "h_out", "hh_out", "hl_out"))
        proj_out = sem("proj_out")
        swapped, rope_cos, rope_out = sem("swapped"), sem("rope_cos"), sem("rope_out")
        pool_win, pooled_out, pool_mm, pool_hi, pool_lo = (
            sem(n) for n in ("pool_win", "pooled_out", "pool_mm", "pool_hi", "pool_lo"))
        pool_step = sem("pool_step")
        st_mm, st_out, o_mm, o_out, osq_out = (sem(n) for n in ("st_mm", "st_out", "o_mm", "o_out", "osq_out"))
        hms_ready, hdiag_ready, hspread_ready = (sem(n) for n in ("hms_ready", "hdiag_ready", "hspread_ready"))
        gate_tanh, head_out, head_hi, head_lo = (
            sem(n) for n in ("gate_tanh", "head_out", "head_hi", "head_lo"))
        bias_in, conv_in, cw2_in, wg_in, sink_in = (
            sem(n) for n in ("bias_in", "conv_in", "cw2_in", "wg_in", "sink_in"))
        bias_mm, bias_row, bias_written, bias_ready = (
            sem(n) for n in ("bias_mm", "bias_row", "bias_written", "bias_ready"))
        y_ready, wg_split, gate_mm, gate_raw, half_ready = (
            sem(n) for n in ("y_ready", "wg_split", "gate_mm", "gate_raw", "half_ready"))
        proj2, key_swapped, kz_zero, kz_direct, kz_ready = (
            sem(n) for n in ("proj2", "key_swapped", "kz_zero", "kz_direct", "kz_ready"))
        ga_tanh = sem("ga_tanh")
        score_mm, logit_out, neg_max, exp_out, prob_turned, prob_t_out, pv_mm, y_taken = (
            sem(n) for n in ("score_mm", "logit_out", "neg_max", "exp_out", "prob_turned", "prob_t_out", "pv_mm",
                             "y_taken"))
        sink_gap, sink_exp = sem("sink_gap"), sem("sink_exp")
        blk_zero, blk_ready, blk_hi, blk_lo = (sem(n) for n in ("blk_zero", "blk_ready", "blk_hi", "blk_lo"))
        hid_z_ready, hid_tanh, hid_ready, hid_taken = (
            sem(n) for n in ("hid_z_ready", "hid_tanh", "hid_ready", "hid_taken"))
        cmp_mm, kcz_ready, vblk_ready, cscore_mm, clogit, cexp, cprob, cturned, cprob_t, cout_mm = (
            sem(n) for n in ("cmp_mm", "kcz_ready", "vblk_ready", "cscore_mm", "clogit", "cexp", "cprob",
                             "cturned", "cprob_t", "cout_mm"))
        y_turned, y_hi, y_lo = (sem(n) for n in ("y_turned", "y_hi", "y_lo"))
        up_out, merged, merged_hi, merged_lo = (sem(n) for n in ("up_out", "merged", "merged_hi", "merged_lo"))
        conv_0, conv_1, conv_2 = sem("conv_0"), sem("conv_1"), sem("conv_2")
        out_turned, out_copied = sem("out_turned"), sem("out_copied")
        out_written = sem("out_written")

        def raw_count(u):
            return 16 * (u // SLOTS + 1)

        w_rows = lambda w, r0: w[r0:r0 + 2 * P, :].rearrange("(k p) n -> p k n", p=P)

        def w_cols(w):
            return w.rearrange("(k p) n -> p k n", p=P)

        def k_n(tile, k):
            return tile.rearrange("p (k n) -> p k n", k=k)

        block = ctx.enter_context(nc.Block())

        @block.sync
        def _(sp):

            def unit(u, src, k, slot=None, count=None):
                slot = u % SLOTS if slot is None else slot
                if count is None:
                    count = u - 2
                if not isinstance(count, int) or count > 0:
                    sp.wait_ge(lo_done, count)
                sp.dma_start(k_n(raw[:, slot], k), src).then_inc(raw_in[slot], 16)

            def ffn(base, w1, off1, w3, off3, w2):
                c1, c3 = w_cols(w1)[:, :, off1:off1 + FF], w_cols(w3)[:, :, off3:off3 + FF]
                r2 = w2.rearrange("(k p) n -> p k n", p=P)
                unit(base, c1[:, :, 0:UC], DC)
                unit(base + 1, c3[:, :, 0:UC], DC)
                unit(base + 2, c1[:, :, UC:2 * UC], DC)
                unit(base + 3, c3[:, :, UC:2 * UC], DC)
                unit(base + 4, r2[:, 0:2, :], 2)
                c1, c3 = c1[:, :, UC:], c3[:, :, UC:]
                with sp.Fori(2, FI) as i:
                    unit(None, c1[:, :, bass.ds((i - 1) * UC, UC)], DC, (base + 2) % SLOTS, i * 3 + (base - 3))
                    unit(None, c3[:, :, bass.ds((i - 1) * UC, UC)], DC, base % SLOTS, i * 3 + (base - 2))
                    unit(None, r2[:, bass.ds(i * 2 - 2, 2), :], 2, (base + 1) % SLOTS, i * 3 + (base - 1))
                unit(base + 3 * FI - 1, r2[:, 2 * FI - 2:2 * FI, :], 2)

            ffn(U_FFN1, a["ffn1_w1"][0], 0, a["ffn1_w3"][0], 0, a["ffn1_w2"][0])
            w_in = w_cols(a["w_in"][0])
            for m in range(10):
                unit(U_MIX + m, w_in[:, :, m * UC:(m + 1) * UC], DC)
            for m in range(4):
                unit(U_OUT1 + m, w_rows(a["w_out"][0], 2 * P * m), 2)
            ffn(U_FFN2, a["ffn2_w1"][0], 0, a["ffn2_w3"][0], 0, a["ffn2_w2"][0])
            w2 = w_cols(a["w_in_2"][0])
            for m in range(20):
                if m in CW:
                    src = a["cmp_w1_k_2" if m < CW[2] else "cmp_w1_v_2"][0]
                    src = src.rearrange("(j p) n -> p j n", p=P)[:, 8 * (m % 2):8 * (m % 2) + 8]
                else:
                    c0 = m * UC if m < 8 else 2072 + (m - 8) * UC if m < 14 else 3096 + (m - 16) * UC
                    src = w2[:, :, c0:c0 + UC]
                unit(U_IN2 + m, src, DC)
            for m in range(4):
                src = w_cols(a["w_up_a_2" if m < 2 else "w_up_b_2"][0])
                unit(U_UP + m, src[:, :, (m % 2) * 512:(m % 2 + 1) * 512], 4)
            for m in range(4):
                unit(U_OUT2 + m, w_rows(a["w_out_2"][0], 2 * P * m), 2)
            wf = a["w_ffn_in_2"][0]
            ffn(U_FFN3, wf, FF, wf, 0, a["w_ffn_out_2"][0])
            sp.wait_ge(out_copied, 4)
            for tt in range(2):
                sp.dma_start(out[0, tt * P:(tt + 1) * P, :], out_s[:, tt]).then_inc(out_written, 16)
            sp.wait_ge(out_written, 32)

        @block.scalar
        def _(act):
            act.dma_start(cst[:], a["c_small"]).then_inc(first_in, 16)
            act.dma_start(x_tok, a["x"][0].rearrange("(t p) n -> p t n", p=P)).then_inc(first_in, 16)
            act.wait_ge(vec_zero, 1)
            for col, name in ((V_FFN1, "ffn1_norm"), (V_MIX, "mix_norm"), (V_FFN2, "ffn2_norm"),
                              (V_MIX2, "norm_mix_2"), (V_FFN3, "norm_ffn_2"),
                              (V_POOL, "pool_scale"), (V_RET, "ret_norm")):
                v = rows8(a[name][0])
                act.dma_start(vec_rows[col:col + v.shape[0], :], v).then_inc(first_in, 16)
            for col, name in ((V_FINAL, "final_norm"), (V_FINAL2, "norm_final_2")):
                act.dma_start(vec_rows[col:col + DC, :], rows8(a[name])).then_inc(first_in, 16)
            for col, name in ((V_POSK, "cmp_pos_k_2"), (V_POSV, "cmp_pos_v_2")):
                act.dma_start(vec_rows[col:col + 16, :],
                              a[name][0].rearrange("(j s) d -> j (s d)", s=2)).then_inc(first_in, 16)

            act.dma_start(oh, a["c_onehot"]).then_inc(bias_in, 16)
            act.dma_start(bias_mask, a["c_mask"]).then_inc(bias_in, 16)
            act.dma_start(bias_table, a["rel_bias_table_2"]).then_inc(bias_in, 16)
            for j in range(3):
                act.dma_start(conv_rows[:, j], rows8(a["conv_w_2"][0, j])).then_inc(conv_in, 16)
            act.dma_start(conv_rows[:, 3], rows8(a["conv_b_2"][0])).then_inc(conv_in, 16)
            act.dma_start(sink[:], a["attn_sinks_2"][0].partition_broadcast(P)).then_inc(sink_in, 16)
            act.dma_start(wg_raw, w_cols(a["w_in_2"][0])[:, :, 2048:2072]).then_inc(wg_in, 16)

            def hi(u):
                act.wait_ge(raw_in[u % SLOTS], raw_count(u))
                if u >= SLOTS:
                    act.wait_ge(unit_done, u - 2)
                nc.scalar.activation(w_hi[:, u % SLOTS], raw[:, u % SLOTS], ACT.Copy).then_inc(hi_done, 1)

            def hi_in_loop(i, base, c):
                s = (base + c) % SLOTS
                act.wait_ge(raw_in[s], i * 16 + 16 * ((base + c) // SLOTS + 1))
                act.wait_ge(unit_done, i * 3 + (base + c - 2))
                nc.scalar.activation(w_hi[:, s], raw[:, s], ACT.Copy).then_inc(hi_done, 1)

            def handoff(n, nh, gain):
                for c in range(DC):
                    act.wait_ge(x_ready, DC * n + c + 1)
                    nc.scalar.activation(xh[:, c], x[:, c], ACT.Copy, scale=vec[:, gain + c:gain + c + 1]) \
                        .then_inc(xh_ready, 1)

            def ffn(f, base):
                n0 = FI * f

                def tanh(i):
                    act.wait_ge(a_out, i + (n0 + 1))
                    nc.scalar.activation(t_s, a_s, ACT.Tanh, scale=0.5).then_inc(tanh_out, 1)

                def h_hi(i, w2_before):
                    act.wait_ge(h_out, i + (n0 + 1))
                    if w2_before is not None:
                        act.wait_ge(unit_done, w2_before)
                    nc.scalar.activation(hh[:].rearrange("p a t -> p (a t)"), h_s, ACT.Copy).then_inc(hh_out, 1)

                hi(base + 2)
                tanh(0)
                hi(base + 3)
                h_hi(0, None)
                with act.Fori(1, FI) as i:
                    hi_in_loop(i, base, 1)
                    tanh(i)
                    hi_in_loop(i, base, 2)
                    hi_in_loop(i, base, 3)
                    h_hi(i, i * 3 + (base + 2))
                hi(base + 3 * FI + 1)

            hi(0)
            hi(1)
            act.wait_ge(vec_ready, 1)
            handoff(0, 0, V_FFN1)
            act.wait_ge(bias_row, 1)
            act.dma_start(scratch, bias_rows).then_inc(bias_written, 16)
            ffn(0, U_FFN1)
            act.dma_start(table, a["c_table"]).then_inc(table_in, 16)
            act.dma_start(pool_ws, a["pool_w"][0].rearrange("g k n -> k g n")).then_inc(pw_in, 16)
            handoff(1, 1, V_MIX)
            def o_copy(j):
                act.wait_ge(o_mm, j + 1)
                nc.scalar.activation(o_s[:, 2 * j:2 * j + 2], halves(wk[:, 2 + j]), ACT.Copy).then_inc(o_out, 1)

            def pool_hi_part(j):
                for g in (2 * j, 2 * j + 1):
                    act.wait_ge(pool_mm, j + 1)
                    nc.scalar.activation(mh[:, g], acc[:, j, (g % 2) * T:(g % 2 + 1) * T], ACT.Copy,
                                         scale=vec[:, V_POOL + g:V_POOL + g + 1]).then_inc(pool_hi, 1)

            def gate(j):
                act.wait_ge(proj_out, 9 + j)
                nc.scalar.activation(g_t[:, j], g_s[:, j], ACT.Tanh, scale=0.5).then_inc(gate_tanh, 1)

            for m in range(10):
                hi(U_MIX + m + 2)
                if m == 7:
                    pool_hi_part(0)
                if m == 8:
                    pool_hi_part(1)
            gate(0)
            o_copy(0)
            gate(1)
            o_copy(1)
            hi(U_OUT1 + 2)
            hi(U_OUT1 + 3)
            for j in range(2):
                act.wait_ge(head_out, j + 1)
                nc.scalar.activation(mh[:, 4 + 2 * j:6 + 2 * j], b_h[:, 2 * j:2 * j + 2], ACT.Copy) \
                    .then_inc(head_hi, 1)
            hi(U_OUT1 + 4)
            hi(U_OUT1 + 5)
            handoff(2, 2, V_FFN2)
            ffn(1, U_FFN2)
            handoff(4, 3, V_MIX2)
            act.wait_ge(wg_in, 16)
            nc.scalar.activation(wg_hi[:], wg_raw, ACT.Copy).then_inc(wg_split, 1)

            def attend(k):
                for s in range(SLOTS_A):
                    if slot_time(s) + 1 == k:
                        act.wait_ge(prob_turned, s + 1)
                        if s >= 2:
                            act.wait_ge(pv_mm, s - 1)
                        nc.scalar.activation(prob_t[s % 2], acc[:, 2 + s % 2], ACT.Copy).then_inc(prob_t_out, 1)
                for s in range(SLOTS_A):
                    if slot_time(s) == k:
                        r, w = divmod(s, 6)
                        nh, h0, b = (2, 2 * w, 1) if w < 4 else (4, 4 * (w - 4), 0)
                        act.wait_ge(neg_max, s + 1)
                        if s >= 2:
                            act.wait_ge(prob_turned, s - 1)
                        n = 512 // nh
                        for h in range(nh):
                            cols = slice(h * n, (h + 1) * n)
                            ex = nc.scalar.activation(prob[s % 2][:, cols], logit[s % 2][:, cols], ACT.Exp,
                                                      bias=nmx[:, r, b, h0 + h:h0 + h + 1],
                                                      accum_out=sums[:, r, b, h0 + h:h0 + h + 1])
                        ex.then_inc(exp_out, 1)

            def key_halves(n):
                act.wait_ge(key_swapped, (1, 3, 4)[n])
                act.wait_ge(kz_zero, 2)
                if n == 2:
                    act.wait_ge(score_mm, 6)
                z, bank = kz[n % 2], acc[:, (0, 0, 1)[n]]
                nc.scalar.activation(z[0:HD, 1, 0], bank[0:HD, 0:T], ACT.Copy)
                nc.scalar.activation(z[HD:P, 0, 1], bank[HD:P, 0:T], ACT.Copy).then_inc(kz_ready, 1)

            def y_hi_part(n):
                act.wait_ge(y_turned, n + 1)
                c0, b = 4 * (n // 2), n % 2
                bank = acc[:, 2 + b] if n < 2 else acc[:, b]
                nc.scalar.activation(mh[:, c0:c0 + 4, b * P:(b + 1) * P], k_n(bank, 4), ACT.Copy).then_inc(y_hi, 1)

            def gate_tanhs(j, n_out):
                act.wait_ge(proj2, n_out)
                buf = (ga if j < 4 else gb)[:, 2 * (j % 4):2 * (j % 4) + 2]
                nc.scalar.activation(buf, buf, ACT.Tanh, scale=0.5).then_inc(ga_tanh, 1)

            for m in range(20):
                if m == 2:
                    act.wait_ge(gate_mm, 1)
                    act.wait_ge(half_ready, 1)
                    for tt in range(2):
                        g = nc.scalar.activation(gates[:, tt], wk[:, 3, tt * 32:tt * 32 + 24], ACT.Tanh,
                                                 scale=half_r[:, tt:tt + 1])
                    g.then_inc(gate_raw, 1)
                for half in range(2):
                    k = position_time(m, half)
                    if k is not None:
                        attend(k)
                    if (m, half) == (19, 0):
                        act.wait_ge(hid_z_ready, 1)
                        nc.scalar.activation(hid_t, hid_z, ACT.Tanh, scale=0.7978845608028654).then_inc(hid_tanh, 1)
                    if half == 0:
                        hi(U_IN2 + m + 2)
                    if (m, half) == (3, 1):
                        key_halves(0)
                    if (m, half) == (7, 1):
                        act.wait_ge(blk_ready, 1)
                        nc.scalar.activation(blk_hl[0], blk, ACT.Copy).then_inc(blk_hi, 1)
                    if (m, half) == (8, 0):
                        key_halves(1)
                        key_halves(2)
                    if half == 1 and 9 <= m < 15:
                        gate_tanhs(m - 9, m)
                    if (m, half) == (17, 0):
                        y_hi_part(0)
                        y_hi_part(1)
                    if k == 7:
                        act.wait_ge(sink_gap, 1)
                        nc.scalar.activation(mx[:, 0], mx[:, 0], ACT.Exp).then_inc(sink_exp, 1)
            hi_next = U_UP + 2
            gate_tanhs(6, 15)
            act.wait_ge(cmp_mm, 1)
            act.wait_ge(kz_zero, 3)
            nc.scalar.activation(kcz[0:HD, 0], acc[0:HD, 0, 0:32], ACT.Copy)
            nc.scalar.activation(kcz[HD:P, 1], acc[HD:P, 0, 0:32], ACT.Copy).then_inc(kcz_ready, 1)
            act.wait_ge(clogit, 1)
            nc.scalar.activation(prob_c[:, :, 0:NCMP], prob_c[:, :, 0:NCMP], ACT.Exp).then_inc(cexp, 1)
            gate_tanhs(7, 16)
            hi(hi_next)
            act.wait_ge(cturned, 1)
            nc.scalar.activation(prob_ct, k_n(acc[:, 3, 0:T], 2), ACT.Copy).then_inc(cprob_t, 1)
            hi(hi_next + 1)
            y_hi_part(2)
            y_hi_part(3)
            hi(hi_next + 2)
            hi(hi_next + 3)
            for j in range(2):
                act.wait_ge(merged, j + 1)
                nc.scalar.activation(xh[:, 4 * j:4 * j + 4], ga[:, 4 * j:4 * j + 4], ACT.Copy).then_inc(merged_hi, 1)
            for u in range(U_OUT2 + 2, U_OUT2 + 6):
                hi(u)
            handoff(5, 4, V_FFN3)

            def conv_start(i, n, src, dst, f0, out_sem):
                act.wait_ge(out_sem, i + (2 * FI + 1))
                for t in range(2):
                    f = f0 + t + i * 2
                    nc.scalar.activation(k_n(dst, 2)[:, t], k_n(src, 2)[:, t], ACT.Identity,
                                         scale=conv[:, 2, bass.ds(f, 1)], bias=conv[:, 3, bass.ds(f, 1)]) \
                        .then_inc(conv_0, 1)

            def ffn3_step(i, last):
                n0 = 2 * FI
                if i is not None and not (isinstance(i, int) and i == 0):
                    hi_in_loop(i, U_FFN3, 1)
                else:
                    hi(U_FFN3 + 2)
                conv_start(i, 0, a_s, conv_a, 22, a_out)
                if isinstance(i, int) and i == 0:
                    hi(U_FFN3 + 3)
                else:
                    hi_in_loop(i, U_FFN3, 2)
                act.wait_ge(conv_2, i * 4 + 2)
                nc.scalar.activation(t3_s, conv_a, ACT.Tanh, scale=0.5).then_inc(tanh_out, 1)
                conv_start(i, 1, b_s, conv_b, 0, b_out)
                if not (isinstance(i, int) and i == 0) and not last:
                    hi_in_loop(i, U_FFN3, 3)
                act.wait_ge(h_out, i + (n0 + 1))
                if not (isinstance(i, int) and i == 0):
                    act.wait_ge(unit_done, i * 3 + (U_FFN3 + 2))
                nc.scalar.activation(hh[:].rearrange("p a t -> p (a t)"), h3_s, ACT.Copy).then_inc(hh_out, 1)

            ffn3_step(0, False)
            with act.Fori(1, FI - 1) as i:
                ffn3_step(i, False)
            ffn3_step(FI - 1, True)
            for n in (0, 2):
                act.wait_ge(out_turned, n + 1)
                nc.scalar.activation(out_s[:, n // 2, 0:512], acc[:, n], ACT.Copy).then_inc(out_copied, 1)

        @block.gpsimd
        def _(pool):
            nc.gpsimd.memset(vec_rows, 0.0).then_inc(vec_zero, 1)
            nc.gpsimd.memset(ones[:], 1.0).then_inc(const_set, 1)
            nc.gpsimd.memset(mean_d[:], 1.0 / D).then_inc(const_set, 1)
            nc.gpsimd.memset(mean_h[:], 1.0 / P).then_inc(const_set, 1)
            nc.gpsimd.memset(zeros[:], 0.0).then_inc(const_set, 1)

            def squares(n):
                for c in range(DC):
                    pool.wait_ge(x_ready, DC * n + c + 1)
                    nc.gpsimd.tensor_tensor(sq[:, c], x[:, c], x[:, c], ALU.mult).then_inc(sq_ready, 1)

            squares(0)
            squares(1)
            steps = [0]

            def step(ins):
                ins.then_inc(pool_step, 1)
                steps[0] += 1
                pool.wait_ge(pool_step, steps[0])

            for buf in (pool_u, win_a, win_b):
                nc.gpsimd.memset(buf[:, :, 0:PAD], 0.0).then_inc(pool_step, 1)
                steps[0] += 1
            pool.wait_ge(pool_step, steps[0])
            pool.wait_ge(proj_out, 2)
            for g0, by, src, dst in ((0, 1, pool_u, win_a), (1, 2, win_a, win_b), (2, 4, win_b, win_a),
                                     (3, 8, win_a, win_b)):
                last = nc.gpsimd.tensor_tensor(dst[:, g0:, by:], src[:, g0:, by:], src[:, g0:, 0:PAD + T - by],
                                               ALU.add)
                if g0 < 3:
                    step(last)
                else:
                    last.then_inc(pool_win, 1)
            pool.wait_ge(table_in, 16)
            for j, (src, dst) in enumerate(((q_s, q_r), (q_s, q_r), (k_s, k_r), (k_s, k_r))):
                pool.wait_ge(proj_out, 3 + j)
                h = 2 * (j % 2)
                nc.gpsimd.tensor_tensor(dst[:, h:h + 2], src[:, h:h + 2], bcast(table[:, T_COS:T_COS + T], 2),
                                        ALU.mult).then_inc(rope_cos, 1)
            for j in range(2):
                pool.wait_ge(o_out, j + 1)
                nc.gpsimd.tensor_tensor(o_sq[:, 2 * j:2 * j + 2], o_s[:, 2 * j:2 * j + 2],
                                        o_s[:, 2 * j:2 * j + 2], ALU.mult).then_inc(osq_out, 1)
            squares(2)
            pool.wait_ge(bias_written, 16)
            nc.gpsimd.dma_start(bias, bass.AP(tensor=scratch.tensor, offset=0,
                                              ap=[[1, P], [BIASW, 16], [1, T]])).then_inc(bias_ready, 16)
            for z in kz:
                nc.gpsimd.memset(z, 0.0).then_inc(kz_zero, 1)
            nc.gpsimd.memset(blk, 0.0).then_inc(blk_zero, 1)
            squares(3)
            squares(4)

            def key_direct(n, n_out):
                pool.wait_ge(proj2, n_out)
                if n == 2:
                    pool.wait_ge(score_mm, 6)
                pool.wait_ge(kz_zero, 2)
                nc.gpsimd.tensor_copy(kz[n % 2][0:HD, 0, 0], kf[0:HD, n]).then_inc(kz_direct, 1)
                pool.wait_ge(kz_direct, 2 * n + 1)
                nc.gpsimd.tensor_copy(kz[n % 2][HD:P, 1, 1], kf[HD:P, n]).then_inc(kz_direct, 1)
                pool.wait_ge(kz_direct, 2 * n + 2)

            pool.wait_ge(sq_ready, 5 * DC)
            key_direct(0, 3)
            key_direct(1, 7)
            key_direct(2, 8)
            nc.gpsimd.memset(kcz, 0.0).then_inc(kz_zero, 1)
            nc.gpsimd.memset(prob_c, 0.0).then_inc(kz_zero, 1)
            pool.wait_ge(key_swapped, 4)
            pool.wait_ge(kz_direct, 6)
            for c0, name in ((0, "cmp_w2_k_2"), (HD, "cmp_w2_k_2"), (2 * HD, "cmp_w2_v_2")):
                nc.gpsimd.dma_start(cmp_w2[:, :, c0:c0 + HD], w_cols(a[name][0])).then_inc(cw2_in, 16)
            squares(5)
            squares(6)

        @block.vector
        def _(dve):
            steps = [0]

            def step(ins):
                ins.then_inc(dve_step, 1)
                steps[0] += 1
                dve.wait_ge(dve_step, steps[0])

            def lo(u):
                dve.wait_ge(hi_done, u + 1)
                s = u % SLOTS
                nc.vector.tensor_tensor(w_lo[:, s], raw[:, s], w_hi[:, s].bitcast(F32), ALU.subtract) \
                    .then_inc(lo_done, 1)

            def lo_in_loop(i, base, c):
                s = (base + c) % SLOTS
                dve.wait_ge(hi_done, i * 3 + (base + c + 1))
                nc.vector.tensor_tensor(w_lo[:, s], raw[:, s], w_hi[:, s].bitcast(F32), ALU.subtract) \
                    .then_inc(lo_done, 1)

            def x_lo(c, nh, gain):
                dve.wait_ge(xh_ready, DC * nh + c + 1)
                nc.vector.scalar_tensor_tensor(out=xl[:, c], in0=x[:, c], scalar=vec[:, gain + c:gain + c + 1],
                                               in1=xh[:, c].bitcast(F32), op0=ALU.mult, op1=ALU.subtract) \
                    .then_inc(xl_ready, 1)

            def add_residual(c, na, coef):
                dve.wait_ge(acc_ready, DC * na + c // 2 * 2 + 2)
                if coef is None:
                    nc.vector.tensor_copy(x[:, c], acc_tile(c)).then_inc(x_ready, 1)
                else:
                    nc.vector.scalar_tensor_tensor(out=x[:, c], in0=acc_tile(c), scalar=coef, in1=x[:, c],
                                                   op0=ALU.mult, op1=ALU.add).then_inc(x_ready, 1)

            def handoff(na, nh, coef, gain):
                for c in range(DC + 1):
                    if c < DC:
                        add_residual(c, na, coef)
                    if c:
                        x_lo(c - 1, nh, gain)

            def rsqrt(src, n):
                v, r, t = (nr[:, j, 0:n] for j in range(3))
                step(nc.vector.tensor_scalar(v, src, EPS, None, ALU.add))
                step(nc.vector.tensor_scalar(r.bitcast(I32), v.bitcast(I32), 1, None, ALU.logical_shift_right))
                step(nc.vector.tensor_scalar(r.bitcast(I32), r.bitcast(I32), -1.0, float(0x5F3759DF),
                                             ALU.mult, ALU.add))
                for _ in range(4):
                    step(nc.vector.scalar_tensor_tensor(out=t, in0=r, scalar=-0.5, in1=r, op0=ALU.mult, op1=ALU.mult))
                    step(nc.vector.tensor_tensor(t, t, v, ALU.mult))
                    step(nc.vector.scalar_tensor_tensor(out=r, in0=t, scalar=1.5, in1=r, op0=ALU.add, op1=ALU.mult))
                return r

            def rstd(n):
                dve.wait_ge(ms_ready, n + 1)
                r = rsqrt(wk[:, 3, 0:2], 2)
                step(nc.vector.tensor_copy(rstd_t[:], r))
                for tt in range(2):
                    nc.vector.tensor_scalar(diag[:, tt], ident, rstd_t[:, tt:tt + 1], None, ALU.mult) \
                        .then_inc(diag_ready, 1)
                dve.wait_ge(spread_ready, n + 1)
                nc.vector.tensor_copy(rstd_b[:], wk[:, 3, T:2 * T]).then_inc(rstd_ready, 1)
                dve.wait_ge(rstd_ready, n + 1)

            def ffn(f, base, nstat):
                n0 = FI * f

                def a_part(i, unit_end):
                    dve.wait_ge(unit_done, unit_end)
                    nc.vector.tensor_tensor(k_n(a_s, 2), halves(wk[:, 0]), bcast(rstd_b[:], 2), ALU.mult) \
                        .then_inc(a_out, 1)

                def b_part(i, unit_end):
                    dve.wait_ge(unit_done, unit_end)
                    nc.vector.tensor_tensor(k_n(b_s, 2), halves(wk[:, 1]), bcast(rstd_b[:], 2), ALU.mult) \
                        .then_inc(b_out, 1)
                    dve.wait_ge(tanh_out, i + (n0 + 1))
                    nc.vector.scalar_tensor_tensor(out=a_s, in0=t_s, scalar=1.0, in1=a_s, op0=ALU.add,
                                                   op1=ALU.mult).then_inc(h1_out, 1)
                    dve.wait_ge(h1_out, i + (n0 + 1))
                    dve.wait_ge(b_out, i + (n0 + 1))
                    nc.vector.tensor_tensor(h_s, a_s, b_s, ALU.mult).then_inc(h_out, 1)

                def h_lo(i):
                    dve.wait_ge(hh_out, i + (n0 + 1))
                    nc.vector.tensor_tensor(hl[:].rearrange("p a t -> p (a t)"), h_s,
                                            hh[:].bitcast(F32).rearrange("p a t -> p (a t)"), ALU.subtract) \
                        .then_inc(hl_out, 1)

                lo(base + 2)
                rstd(nstat)
                a_part(0, base + 1)
                lo(base + 3)
                b_part(0, base + 2)
                h_lo(0)
                with dve.Fori(1, FI) as i:
                    lo_in_loop(i, base, 1)
                    a_part(i, i * 3 + base)
                    lo_in_loop(i, base, 2)
                    b_part(i, i * 3 + (base + 1))
                    lo_in_loop(i, base, 3)
                    h_lo(i)
                lo(base + 3 * FI + 1)

            dve.wait_ge(vec_turned, 1)
            nc.vector.tensor_copy(vec[:], wk[:, 0, 0:V_COLS]).then_inc(vec_ready, 1)
            dve.wait_ge(vec_ready, 1)
            nc.vector.tensor_copy(conv[:], wk[:, 0, 96:96 + 176].rearrange("p (j f) -> p j f", j=4)) \
                .then_inc(vec_ready, 1)
            handoff(0, 0, None, V_FFN1)
            dve.wait_ge(bias_mm, 1)
            nc.vector.tensor_tensor(bias_rows, wk[0:16, 1, 0:BIASW], bias_mask, ALU.add).then_inc(bias_row, 1)
            dve.wait_ge(bias_mm, 2)
            for b in range(2):
                cols = slice(C_NEGC + b * NCMP, C_NEGC + (b + 1) * NCMP)
                step(nc.vector.tensor_tensor(bias_c[:, b], wk[:, 2, 120 * b:120 * b + 120]
                                             .rearrange("p (c h) -> p h c", h=NHA), bcast(cst[:, cols], NHA), ALU.add))
            lo(0)
            lo(1)
            ffn(0, U_FFN1, 0)
            handoff(1, 1, 0.25, V_MIX)

            def table_bc(c0, n):
                return bcast(table[:, c0:c0 + T], n)

            def proj(m):
                dve.wait_ge(unit_done, U_MIX + m + 1)
                src = halves(wk[:, m % 2])
                j = 2 * (m % 2)
                if m in (6, 7):
                    for tt in range(2):
                        last = nc.vector.tensor_scalar(v_t[:, tt, j * P:(j + 2) * P], src[:, tt],
                                                       rstd_t[:, tt:tt + 1], None, ALU.mult)
                    last.then_inc(proj_out, 1)
                    return
                if m in (8, 9):
                    dst = k_n(g_s[:, m - 8], 2)
                elif m < 2:
                    dst = pool_u[:, j:j + 2, PAD:]
                else:
                    dst = (q_s if m < 4 else k_s)[:, j:j + 2]
                nc.vector.tensor_tensor(dst, src, bcast(rstd_b[:], 2), ALU.mult).then_inc(proj_out, 1)

            def rope(j):
                dst, h = (q_r, k_r)[j // 2], 2 * (j % 2)
                tmp = k_n(work[:, 4], 2)
                dve.wait_ge(swapped, j + 1)
                step(nc.vector.tensor_tensor(tmp, halves(acc[:, j]), table_bc(T_SIN, 2), ALU.mult))
                dve.wait_ge(rope_cos, j + 1)
                nc.vector.tensor_tensor(dst[:, h:h + 2], dst[:, h:h + 2], tmp, ALU.add).then_inc(rope_out, 1)
                dve.wait_ge(rope_out, j + 1)

            def pool_mean():
                dve.wait_ge(pool_win, 1)
                dve.wait_ge(table_in, 16)
                rc = table[:, T_RC:T_RC + 4 * T].rearrange("p (g t) -> p g t", g=4)
                for g, win in enumerate((win_a, win_b, win_a, win_b)):
                    last = nc.vector.tensor_tensor(pooled[:, g], win[:, g, PAD:], rc[:, g], ALU.mult)
                step(last)
                nc.vector.tensor_tensor(pooled, pooled, pool_u[:, :, PAD:], ALU.subtract).then_inc(pooled_out, 1)

            def pool_lo_part(j):
                for g in (2 * j, 2 * j + 1):
                    dve.wait_ge(pool_hi, 2 * j + 2)
                    nc.vector.scalar_tensor_tensor(out=ml[:, g], in0=acc[:, j, (g % 2) * T:(g % 2 + 1) * T],
                                                   scalar=vec[:, V_POOL + g:V_POOL + g + 1],
                                                   in1=mh[:, g].bitcast(F32), op0=ALU.mult, op1=ALU.subtract) \
                        .then_inc(pool_lo, 1)

            def decay(h):
                dve.wait_ge(st_mm, h + 1)
                nc.vector.tensor_tensor(st[:, h], acc[:, 2 + h % 2, 0:DEC],
                                        table[:, T_DEC + h * DEC:T_DEC + (h + 1) * DEC], ALU.mult) \
                    .then_inc(st_out, 1)

            for m in range(10):
                lo(U_MIX + m + 2)
                if m == 0:
                    rstd(1)
                proj(m)
                if m == 4:
                    pool_mean()
                    rope(0)
                if m == 5:
                    rope(1)
                if m == 6:
                    rope(2)
                if m == 7:
                    rope(3)
                    pool_lo_part(0)
                if m == 8:
                    pool_lo_part(1)
                    decay(0)
                    decay(1)
                if m == 9:
                    decay(2)
                    decay(3)
            dve.wait_ge(hms_ready, 1)
            r = rsqrt(wk[:, 2, 0:8], 8)
            nc.vector.tensor_tensor(diag_h, bcast(ident, 8), bcast_in(r, P), ALU.mult).then_inc(hdiag_ready, 1)
            for j in range(2):
                dve.wait_ge(gate_tanh, j + 1)
                step(nc.vector.scalar_tensor_tensor(out=g_t[:, j], in0=g_t[:, j], scalar=1.0, in1=g_s[:, j],
                                                    op0=ALU.add, op1=ALU.mult))
            dve.wait_ge(hspread_ready, 1)
            for h in range(HR):
                last = nc.vector.scalar_tensor_tensor(out=b_h[:, h], in0=o_s[:, h],
                                                      scalar=vec[:, V_RET + h:V_RET + h + 1],
                                                      in1=wk[:, h // 2, (h % 2) * T:(h % 2 + 1) * T],
                                                      op0=ALU.mult, op1=ALU.mult)
            step(last)
            for j in range(2):
                pair = b_h[:, 2 * j:2 * j + 2]
                nc.vector.scalar_tensor_tensor(out=pair, in0=pair, scalar=0.5, in1=k_n(g_t[:, j], 2), op0=ALU.mult,
                                               op1=ALU.mult).then_inc(head_out, 1)
            for j in range(2):
                dve.wait_ge(head_hi, j + 1)
                nc.vector.tensor_tensor(ml[:, 4 + 2 * j:6 + 2 * j], b_h[:, 2 * j:2 * j + 2],
                                        mh[:, 4 + 2 * j:6 + 2 * j].bitcast(F32), ALU.subtract).then_inc(head_lo, 1)
            for m in range(4):
                lo(U_OUT1 + m + 2)
            handoff(2, 2, 1.0, V_FFN2)
            ffn(1, U_FFN2, 2)
            for c in range(DC):
                add_residual(c, 3, 0.25)
            rstd(3)
            for c in range(DC + 1):
                if c < DC:
                    nc.vector.scalar_tensor_tensor(out=x[:, c], in0=x[:, c],
                                                   scalar=vec[:, V_FINAL + c:V_FINAL + c + 1], in1=rstd_b[:],
                                                   op0=ALU.mult, op1=ALU.mult).then_inc(x_ready, 1)
                if c:
                    x_lo(c - 1, 3, V_MIX2)

            def proj_2(m):
                dve.wait_ge(unit_done, U_IN2 + m + 1)
                bank = wk[:, m % 2] if m < 14 else wk[:, 19 - m]
                src = halves(bank)
                both = bcast(rstd_b[:], 2)
                if m in (2, 6, 7):
                    n = {2: K_A, 6: K_S, 7: K_W}[m]
                    nc.vector.tensor_tensor(kf[:, n], src[:, 0], rstd_b[:], ALU.mult)
                    if n == K_W:
                        dve.wait_ge(pv_mm, 6)
                    for tt in range(2):
                        last = nc.vector.tensor_scalar(v2[n % 2][:, tt], bank[:, T + tt * P:T + (tt + 1) * P],
                                                       rstd_t[:, tt:tt + 1], None, ALU.mult)
                    last.then_inc(proj2, 1)
                    return
                if m == 5:
                    dst = kf[:, K_CK:K_CV + 1]
                elif m < 2:
                    dst = qa_s[:, 2 * m:2 * m + 2]
                elif m < 5:
                    dst = qb_s[:, 2 * m - 6:2 * m - 4]
                elif m in GA:
                    dst = ga[:, 2 * (m - 8):2 * (m - 8) + 2]
                else:
                    c = 2 * GB.index(m)
                    dst = gb[:, c:c + 2]
                nc.vector.tensor_tensor(dst, src, both, ALU.mult).then_inc(proj2, 1)

            def attend(k):
                for s in range(SLOTS_A):
                    r, w = divmod(s, 6)
                    nh, h0, b = (2, 2 * w, 1) if w < 4 else (4, 4 * (w - 4), 0)
                    if slot_time(s) == k:
                        if s == 0:
                            dve.wait_ge(bias_ready, 16)
                            dve.wait_ge(sink_in, 16)
                        n = 512 // nh
                        hb = h0 + (0 if r == 0 else 8)
                        dve.wait_ge(score_mm, s + 1)
                        if s >= 2:
                            dve.wait_ge(exp_out, s - 1)
                        lg = logit[s % 2].rearrange("p (h n) -> p h n", h=nh)
                        nc.vector.scalar_tensor_tensor(out=lg, in0=acc[:, s % 2].rearrange("p (h n) -> p h n", h=nh),
                                                       scalar=HD ** -0.5, in1=bias[:, hb:hb + nh, 0:n][:, :, ::-1],
                                                       op0=ALU.mult, op1=ALU.add).then_inc(logit_out, 1)
                        dve.wait_ge(logit_out, s + 1)
                        top = mx[:, r, b, h0:h0 + nh]
                        step(nc.vector.tensor_reduce(top, lg, AX_X, ALU.max))
                        if r == 0:
                            step(nc.vector.tensor_tensor(top, top, sink[:, h0:h0 + nh], ALU.max))
                        nc.vector.tensor_scalar(nmx[:, r, b, h0:h0 + nh], top, -1.0, None, ALU.mult) \
                            .then_inc(neg_max, 1)
                for s in range(SLOTS_A):
                    r, w = divmod(s, 6)
                    if slot_time(s) + 2 == k and w in (3, 5):
                        b = 1 if w == 3 else 0
                        if r == 0 and b == 1:
                            continue
                        if r == 0:
                            sinks()
                            for bb in (1, 0):
                                dve.wait_ge(pv_mm, 4 if bb else 6)
                                take_y(0, bb)
                            continue
                        dve.wait_ge(pv_mm, s + 1)
                        take_y(r, b)

            def sinks():
                dve.wait_ge(exp_out, 6)
                for bb in range(2):
                    last = nc.vector.tensor_tensor(mx[:, 0, bb], sink[:], mx[:, 0, bb], ALU.subtract)
                last.then_inc(sink_gap, 1)
                dve.wait_ge(sink_exp, 1)
                step(nc.vector.tensor_tensor(sums[:, 0], sums[:, 0], mx[:, 0], ALU.add))

            def take_y(r, b):
                cf = coef[:, b]
                step(nc.vector.reciprocal(cf, sums[:, r, b]))
                bank = wk[:, 3 - b].rearrange("p (h d) -> p h d", d=HD)
                if r == 0:
                    nc.vector.tensor_tensor(y_a[:, b].rearrange("p (h d) -> p h d", d=HD), bank, bcast_in(cf, HD),
                                            ALU.mult).then_inc(y_taken, 1)
                    return
                g = gates[:, b].rearrange("p (h n) -> p n h", n=3)[:, r]
                step(nc.vector.tensor_tensor(cf, cf, g, ALU.mult))
                dst = y_b[:, b] if r == 1 else y_tmp
                nc.vector.tensor_tensor(dst.rearrange("p (h d) -> p h d", d=HD), bank, bcast_in(cf, HD),
                                        ALU.mult).then_inc(y_taken, 1)
                if r > 1:
                    dve.wait_ge(y_taken, 2 * r + 2 - b)
                    step(nc.vector.tensor_tensor(y_b[:, b], y_b[:, b], y_tmp, ALU.add))

            def blocks():
                dve.wait_ge(key_swapped, 2)
                dve.wait_ge(blk_zero, 1)
                for v in range(2):
                    for g in range(2):
                        for s in range(2):
                            rows = slice(HD * s, HD * (s + 1))
                            src = kf[rows, K_CK + v] if g == s else acc[rows, 0, v * T:(v + 1) * T]
                            src = bass.AP(tensor=src.tensor, offset=src.offset + s,
                                          ap=[list(src.ap[0]), [2, 16], [16, NCMP]])
                            pos = vec[rows, V_POSK + 16 * v:V_POSK + 16 * (v + 1)]
                            last = nc.vector.tensor_tensor(blk[rows, v, :, g * 16:g * 16 + NCMP], src,
                                                           bcast_in(pos, NCMP), ALU.add)
                last.then_inc(blk_ready, 1)

            def y_lo_part(n):
                dve.wait_ge(y_hi, n // 2 * 2 + 2)
                c0, b = 4 * (n // 2), n % 2
                bank = acc[:, 2 + b] if n < 2 else acc[:, b]
                nc.vector.tensor_tensor(ml[:, c0:c0 + 4, b * P:(b + 1) * P], k_n(bank, 4),
                                        mh[:, c0:c0 + 4, b * P:(b + 1) * P].bitcast(F32), ALU.subtract) \
                    .then_inc(y_lo, 1)

            for m in range(20):
                if m == 0:
                    rstd(4)
                    nc.vector.tensor_scalar(half_r[:], rstd_t[:], 0.5, None, ALU.mult).then_inc(half_ready, 1)
                    dve.wait_ge(wg_split, 1)
                    nc.vector.tensor_tensor(wg_lo[:], wg_raw, wg_hi[:].bitcast(F32), ALU.subtract) \
                        .then_inc(wg_split, 1)
                elif m - 1 not in CW:
                    proj_2(m - 1)
                if m == 2:
                    dve.wait_ge(gate_raw, 1)
                    step(nc.vector.tensor_scalar(gates[:], gates[:], 0.5, 0.5, ALU.mult, ALU.add))
                for half in range(2):
                    k = position_time(m, half)
                    if k is not None:
                        attend(k)
                    if half:
                        lo(U_IN2 + m + 2)
                    if (m, half) == (7, 0):
                        blocks()
                    if (m, half) == (8, 0):
                        dve.wait_ge(blk_hi, 1)
                        nc.vector.tensor_tensor(blk_hl[1], blk, blk_hl[0].bitcast(F32), ALU.subtract) \
                            .then_inc(blk_lo, 1)
                if m == 17:
                    y_lo_part(0)
                    y_lo_part(1)
                if m == 18:
                    dve.wait_ge(unit_done, U_IN2 + CW[3] + 1)
                    nc.vector.tensor_copy(hid_x, wk[:, 0, 0:P]).then_inc(hid_taken, 1)
                    dve.wait_ge(hid_taken, 1)
                    step(nc.vector.tensor_tensor(hid_z, hid_x, hid_x, ALU.mult))
                    step(nc.vector.tensor_scalar(hid_z, hid_z, 0.044715, 1.0, ALU.mult, ALU.add))
                    nc.vector.tensor_tensor(hid_z, hid_z, hid_x, ALU.mult).then_inc(hid_z_ready, 1)
                    dve.wait_ge(hid_tanh, 1)
                    step(nc.vector.scalar_tensor_tensor(out=hid_t, in0=hid_t, scalar=1.0, in1=hid_x, op0=ALU.add,
                                                        op1=ALU.mult))
                    nc.vector.tensor_scalar(hid_k, hid_t[:, 0:64].rearrange("p (n m) -> p n m", n=2), 0.5, None,
                                            ALU.mult)
                    for n in range(2):
                        hv = hid_t[:, 64 + 32 * n:96 + 32 * n].rearrange("p (g c) -> p g c", g=2)
                        for g in range(2):
                            last = nc.vector.tensor_scalar(
                                hv_rep[:, n, g * 64:(g + 1) * 64].rearrange("p (r c) -> p r c", r=4),
                                bcast(hv[:, g], 4), 0.5, None, ALU.mult)
                    last.then_inc(hid_ready, 1)
                if m == 19:
                    dve.wait_ge(cmp_mm, 1)
                    nc.vector.tensor_tensor(v_blk, bcast(acc[:, 1, 0:HD], 8),
                                            bcast_in(cst[:, C_BLK:C_BLK + 8], HD), ALU.mult).then_inc(vblk_ready, 1)
                    dve.wait_ge(cscore_mm, 1)
                    dve.wait_ge(kz_zero, 4)
                    for b in range(2):
                        lg = prob_c[:, 8 * b:8 * b + 8, 0:NCMP]
                        src = acc[:, 2, b * P:(b + 1) * P].rearrange("p (h c) -> p h c", c=16)[:, :, 0:NCMP]
                        last = nc.vector.scalar_tensor_tensor(out=lg, in0=src, scalar=HD ** -0.5, in1=bias_c[:, b],
                                                              op0=ALU.mult, op1=ALU.add)
                    step(last)
                    lg = prob_c[:, :, 0:NCMP]
                    step(nc.vector.tensor_reduce(mx_c[:], lg, AX_X, ALU.max))
                    nc.vector.tensor_tensor(lg, lg, bcast_in(mx_c[:], NCMP), ALU.subtract).then_inc(clogit, 1)
                    dve.wait_ge(cexp, 1)
                    step(nc.vector.tensor_reduce(sum_c[:], lg, AX_X, ALU.add))
                    for b in range(2):
                        cols = slice(C_VALC + b * NCMP, C_VALC + (b + 1) * NCMP)
                        last = nc.vector.tensor_tensor(lg[:, 8 * b:8 * b + 8], lg[:, 8 * b:8 * b + 8],
                                                       bcast(cst[:, cols], NHA), ALU.mult)
                    last.then_inc(cprob, 1)
                    step(nc.vector.reciprocal(sum_c[:], sum_c[:]))
                    for b in range(2):
                        g = gates[:, b].rearrange("p (h n) -> p n h", n=3)[:, 0]
                        last = nc.vector.tensor_tensor(sum_c[:, 8 * b:8 * b + 8], sum_c[:, 8 * b:8 * b + 8], g, ALU.mult)
                    step(last)
            proj_2(19)
            lo(U_UP + 2)
            for b in range(2):
                dve.wait_ge(cout_mm, b + 1)
                step(nc.vector.tensor_tensor(y_tmp.rearrange("p (h d) -> p h d", d=HD),
                                             wk[:, 2 + b].rearrange("p (h d) -> p h d", d=HD),
                                             bcast_in(sum_c[:, 8 * b:8 * b + 8], HD), ALU.mult))
                nc.vector.tensor_tensor(y_b[:, b], y_b[:, b], y_tmp, ALU.add).then_inc(y_taken, 1)
                dve.wait_ge(y_taken, 2 * NBR + b + 1)
            lo(U_UP + 3)

            def up(m):
                dve.wait_ge(unit_done, U_UP + m + 1)
                dve.wait_ge(ga_tanh, 2 * m + 2)
                buf = (ga if m < 2 else gb)[:, 4 * (m % 2):4 * (m % 2) + 4]
                banks = wk[:, 2 * (m % 2):2 * (m % 2) + 2].rearrange("p b (h t) -> p (b h) t", t=T)
                nc.vector.scalar_tensor_tensor(out=buf, in0=buf, scalar=1.0, in1=banks, op0=ALU.add,
                                               op1=ALU.mult).then_inc(up_out, 1)
                if m >= 2:
                    dve.wait_ge(up_out, m + 1)
                    both = ga[:, 4 * (m - 2):4 * (m - 2) + 4]
                    nc.vector.tensor_tensor(both, both, buf, ALU.add).then_inc(merged, 1)

            up(0)
            y_lo_part(2)
            y_lo_part(3)
            lo(U_UP + 4)
            up(1)
            lo(U_UP + 5)
            for m in (2, 3):
                up(m)
                cols = slice(4 * (m - 2), 4 * (m - 2) + 4)
                dve.wait_ge(merged_hi, m - 1)
                nc.vector.tensor_tensor(xl[:, cols], ga[:, cols], xh[:, cols].bitcast(F32), ALU.subtract) \
                    .then_inc(merged_lo, 1)
            for u in range(U_OUT2 + 2, U_OUT2 + 6):
                lo(u)
            handoff(4, 4, 0.5, V_FFN3)

            def scaled(i, bank, dst, unit_end, out_sem):
                dve.wait_ge(unit_done, unit_end)
                nc.vector.tensor_tensor(k_n(dst, 2), halves(bank), bcast(rstd_b[:], 2), ALU.mult).then_inc(out_sem, 1)
                dve.wait_ge(out_sem, i + (2 * FI + 1))

            def taps(i, n, src, dst, f0):
                for back, signal, before in ((1, conv_1, conv_0), (2, conv_2, conv_1)):
                    for t in range(2):
                        f = f0 + t + i * 2
                        dve.wait_ge(before, i * 4 + (2 * n + t + 1))
                        tile, new = k_n(src, 2)[:, t], k_n(dst, 2)[:, t, back:]
                        nc.vector.scalar_tensor_tensor(out=new, in0=tile[:, 0:T - back],
                                                       scalar=conv[:, 2 - back, bass.ds(f, 1)], in1=new,
                                                       op0=ALU.mult, op1=ALU.add).then_inc(signal, 1)

            def ffn3_step(i, last):
                n0, base = 2 * FI, U_FFN3
                first = isinstance(i, int) and i == 0
                if first:
                    lo(base + 2)
                    rstd(5)
                else:
                    lo_in_loop(i, base, 1)
                scaled(i, wk[:, 0], a_s, base + 1 if first else i * 3 + base, a_out)
                if first:
                    lo(base + 3)
                else:
                    lo_in_loop(i, base, 2)
                taps(i, 0, a_s, conv_a, 22)
                scaled(i, wk[:, 1], b_s, base + 2 if first else i * 3 + (base + 1), b_out)
                taps(i, 1, b_s, conv_b, 0)
                dve.wait_ge(tanh_out, i + (n0 + 1))
                nc.vector.scalar_tensor_tensor(out=conv_a, in0=t3_s, scalar=1.0, in1=conv_a, op0=ALU.add,
                                               op1=ALU.mult).then_inc(h1_out, 1)
                dve.wait_ge(h1_out, i + (n0 + 1))
                dve.wait_ge(conv_2, i * 4 + 4)
                nc.vector.tensor_tensor(h3_s, conv_a, conv_b, ALU.mult).then_inc(h_out, 1)
                if not first and not last:
                    lo_in_loop(i, base, 3)
                dve.wait_ge(hh_out, i + (n0 + 1))
                nc.vector.tensor_tensor(hl[:].rearrange("p a t -> p (a t)"), h3_s,
                                        hh[:].bitcast(F32).rearrange("p a t -> p (a t)"), ALU.subtract) \
                    .then_inc(hl_out, 1)

            ffn3_step(0, False)
            with dve.Fori(1, FI - 1) as i:
                ffn3_step(i, False)
            ffn3_step(FI - 1, True)
            for c in range(DC):
                add_residual(c, 5, 0.5)
            rstd(6)
            for c in range(DC):
                nc.vector.scalar_tensor_tensor(out=x[:, c], in0=x[:, c],
                                               scalar=vec[:, V_FINAL2 + c:V_FINAL2 + c + 1], in1=rstd_b[:],
                                               op0=ALU.mult, op1=ALU.mult).then_inc(y_ready, 1)
            for n in (1, 3):
                dve.wait_ge(out_turned, n + 1)
                nc.vector.tensor_copy(out_s[:, n // 2, 512:1024], acc[:, n]).then_inc(out_copied, 1)

        @block.tensor
        def _(pe):
            def passes(dst, pairs, start, stop):
                for n, (w, v) in enumerate(pairs):
                    mm = nc.tensor.matmul(dst, w, v, start=start and n == 0, stop=stop and n == len(pairs) - 1,
                                          skip_group_check=True)
                return mm

            def col_tile(slot, t, dst, k=DC, vh=xh, vl=xl, k0=0, arrive=None):
                wh, wl = k_n(w_hi[:, slot], k), k_n(w_lo[:, slot], k)
                cols = slice(t * P, (t + 1) * P)
                for c in range(k):
                    if arrive is not None:
                        pe.wait_ge(arrive[0], arrive[1] + c + 1)
                    mm = passes(dst, ((wh[:, c, cols], vh[:, k0 + c]), (wh[:, c, cols], vl[:, k0 + c]),
                                      (wl[:, c, cols], vh[:, k0 + c])), c == 0, c == k - 1)
                return mm

            def tok_tile(slot, tt, dst, cols):
                wh, wl = k_n(w_hi[:, slot], DC), k_n(w_lo[:, slot], DC)
                rows = slice(tt * P, (tt + 1) * P)
                for c in range(DC):
                    mm = passes(dst, ((xh[:, c, rows], wh[:, c, cols]), (xh[:, c, rows], wl[:, c, cols]),
                                      (xl[:, c, rows], wh[:, c, cols])), c == 0, c == DC - 1)
                return mm

            def open_acc():
                for b in range(4):
                    nc.tensor.matmul(acc[:, b], zeros[:, 0:P], zeros[:], start=True, stop=False,
                                     skip_group_check=True)

            def row_unit(slot, vh, vl, k0, last=False):
                wh, wl = k_n(w_hi[:, slot], 2), k_n(w_lo[:, slot], 2)
                for n in range(DC):
                    cols = slice(n * P, (n + 1) * P)
                    for c in range(2):
                        mm = passes(acc_tile(n), ((wh[:, c, cols], vh[:, k0 + c]), (wh[:, c, cols], vl[:, k0 + c]),
                                                  (wl[:, c, cols], vh[:, k0 + c])), False, last and c == 1)
                    if last:
                        mm.then_inc(acc_ready, 1)
                if last:
                    mm = nc.tensor.matmul(wk[:, 3, 2:4], zeros[:, 0:P], zeros[:, 0:2], start=True, stop=True)
                return mm

            def mean_squares(n):
                pe.wait_ge(sq_ready, DC * (n + 1))
                for tt in range(2):
                    for c in range(DC):
                        mm = nc.tensor.matmul(wk[:, 3, tt:tt + 1], sq[:, c, tt * P:(tt + 1) * P], mean_d[:],
                                              start=c == 0, stop=c == DC - 1)
                mm.then_inc(ms_ready, 1)

            def spread(n):
                pe.wait_ge(diag_ready, 2 * (n + 1))
                for tt in range(2):
                    mm = nc.tensor.matmul(wk[:, 3, T + tt * P:T + (tt + 1) * P], ones[:], diag[:, tt],
                                          start=True, stop=True)
                mm.then_inc(spread_ready, 1)

            def ffn(f, base, nstat, nh, nx):
                n0 = FI * f
                s0, s1, s2 = base % SLOTS, (base + 1) % SLOTS, (base + 2) % SLOTS
                pe.wait_ge(lo_done, base + 1)
                col_tile(s0, 0, wk[:, 0, 0:T], arrive=(xl_ready, DC * nh))
                mean_squares(nstat)
                col_tile(s0, 1, wk[:, 0, T:2 * T]).then_inc(unit_done, 1)
                spread(nstat)
                pe.wait_ge(lo_done, base + 2)
                col_tile(s1, 0, wk[:, 1, 0:T])
                col_tile(s1, 1, wk[:, 1, T:2 * T]).then_inc(unit_done, 1)
                pe.wait_ge(x_ready, DC * (nx + 1))
                open_acc()
                with pe.Fori(1, FI) as i:
                    pe.wait_ge(lo_done, i * 3 + base)
                    pe.wait_ge(a_out, i + n0)
                    col_tile(s2, 0, wk[:, 0, 0:T])
                    col_tile(s2, 1, wk[:, 0, T:2 * T]).then_inc(unit_done, 1)
                    pe.wait_ge(lo_done, i * 3 + (base + 1))
                    pe.wait_ge(b_out, i + n0)
                    col_tile(s0, 0, wk[:, 1, 0:T])
                    col_tile(s0, 1, wk[:, 1, T:2 * T]).then_inc(unit_done, 1)
                    pe.wait_ge(lo_done, i * 3 + (base + 2))
                    pe.wait_ge(hl_out, i + n0)
                    row_unit(s1, hh, hl, 0).then_inc(unit_done, 1)
                pe.wait_ge(lo_done, base + 3 * FI)
                pe.wait_ge(hl_out, n0 + FI)
                row_unit(s2, hh, hl, 0, last=True).then_inc(unit_done, 1)

            pe.wait_ge(const_set, 4)
            pe.wait_ge(first_in, 16 * 13)
            nc.tensor.transpose(wk[:, 0, 0:V_COLS], vec_rows[0:V_COLS], ident[0:V_COLS, 0:V_COLS])
            pe.wait_ge(conv_in, 16 * 4)
            for j in range(4):
                mm = nc.tensor.transpose(wk[:, 0, 96 + 44 * j:96 + 44 * (j + 1)], conv_rows[:, j], ident[0:44, 0:44])
            mm.then_inc(vec_turned, 1)
            for c in range(DC):
                for tt in range(2):
                    mm = nc.tensor.transpose(acc_tile(c)[:, tt * P:(tt + 1) * P], x_tok[:, tt, c * P:(c + 1) * P],
                                             ident)
                mm.then_inc(acc_ready, 1)
            pe.wait_ge(bias_in, 16 * 3)
            nc.tensor.matmul(wk[0:16, 1, 0:BIASW], bias_table, oh[:, OH_D0 - BIAS_D0:OH_D0 - BIAS_D0 + BIASW], start=True, stop=True) \
                .then_inc(bias_mm, 1)
            for n in range(2 * NCMP):
                y0 = OH_D0 + P * (n // NCMP) - 16 * (n % NCMP) - 31
                mm = nc.tensor.matmul(wk[:, 2, 8 * n:8 * n + 8], oh[:, y0:y0 + P], bias_table[:, 8:16],
                                      start=True, stop=True)
            mm.then_inc(bias_mm, 1)
            pe.wait_ge(vec_ready, 2)
            pe.wait_ge(bias_row, 1)
            ffn(0, U_FFN1, 0, 0, 0)

            def swap_halves(j):
                src, h = (q_s, k_s)[j // 2], 2 * (j % 2)
                pe.wait_ge(proj_out, 3 + j)
                if j < 4:
                    nc.tensor.matmul(acc[:, j], swap, src[:, h:h + 2], start=True, stop=True).then_inc(swapped, 1)

            def pool_mix(j):
                pe.wait_ge(pooled_out, 1)
                pe.wait_ge(pw_in, 16)
                pe.wait_ge(rope_out, j + 1)
                for g in (2 * j, 2 * j + 1):
                    mm = nc.tensor.matmul(acc[:, j, (g % 2) * T:(g % 2 + 1) * T], pool_ws[:, g], pooled[:, g],
                                          start=True, stop=True)
                mm.then_inc(pool_mm, 1)

            def scores(h):
                pe.wait_ge(rope_out, 4)
                if h >= 2:
                    pe.wait_ge(st_out, h - 1)
                bank = acc[:, 2 + h % 2]
                nc.tensor.matmul(bank[:, 0:T], k_r[:, h, 0:P], q_r[:, h], start=True, stop=True)
                nc.tensor.matmul(bank[:, T:DEC], k_r[:, h, P:T], q_r[:, h, P:T], start=True, stop=True) \
                    .then_inc(st_mm, 1)

            def head_out_mm(h):
                pe.wait_ge(st_out, h + 1)
                dst = wk[:, 2 + h // 2, (h % 2) * T:(h % 2 + 1) * T]
                nc.tensor.matmul(dst, v_t[:, 0, h * P:(h + 1) * P], st[:, h, 0:T], start=True, stop=False,
                                 skip_group_check=True)
                mm = nc.tensor.matmul(dst[:, P:T], v_t[:, 1, h * P:(h + 1) * P], st[:, h, T:DEC], start=False,
                                      stop=True, skip_group_check=True)
                if h % 2:
                    mm.then_inc(o_mm, 1)

            for m in range(10):
                u = U_MIX + m
                pe.wait_ge(lo_done, u + 1)
                if m >= 2:
                    pe.wait_ge(proj_out, m - 1)
                bank = wk[:, m % 2]
                if m in (6, 7):
                    tok_tile(u % SLOTS, 0, bank[:, 0:T], slice(0, UC))
                    tok_tile(u % SLOTS, 1, bank[:, T:2 * T], slice(0, UC)).then_inc(unit_done, 1)
                else:
                    col_tile(u % SLOTS, 0, bank[:, 0:T], arrive=(xl_ready, DC) if m == 0 else None)
                    if m == 0:
                        mean_squares(1)
                    col_tile(u % SLOTS, 1, bank[:, T:2 * T]).then_inc(unit_done, 1)
                    if m == 0:
                        spread(1)
                if m == 0:
                    pe.wait_ge(x_ready, 2 * DC)
                if m in (3, 4, 5, 6):
                    swap_halves(m - 3)
                if m in (5, 6):
                    pool_mix(m - 5)
                if m == 7:
                    scores(0)
                    scores(1)
                if m == 8:
                    scores(2)
                    scores(3)
                    head_out_mm(0)
                    head_out_mm(1)
            head_out_mm(2)
            head_out_mm(3)
            pe.wait_ge(pool_lo, 4)
            open_acc()
            pe.wait_ge(lo_done, U_OUT1 + 1)
            row_unit(U_OUT1 % SLOTS, mh, ml, 0).then_inc(unit_done, 1)
            pe.wait_ge(osq_out, 2)
            for h in range(HR):
                for tt in range(2):
                    n = 2 * h + tt
                    mm = nc.tensor.matmul(wk[:, 2, n:n + 1], o_sq[:, h, tt * P:(tt + 1) * P], mean_h[:],
                                          start=True, stop=True)
            mm.then_inc(hms_ready, 1)
            pe.wait_ge(lo_done, U_OUT1 + 2)
            row_unit((U_OUT1 + 1) % SLOTS, mh, ml, 2).then_inc(unit_done, 1)
            pe.wait_ge(hdiag_ready, 1)
            pe.wait_ge(proj_out, 10)
            for n in range(8):
                mm = nc.tensor.matmul(wk[:, n // 4, (n % 4) * P:(n % 4 + 1) * P], ones[:], diag_h[:, n],
                                      start=True, stop=True)
            mm.then_inc(hspread_ready, 1)
            pe.wait_ge(head_lo, 2)
            pe.wait_ge(lo_done, U_OUT1 + 3)
            row_unit((U_OUT1 + 2) % SLOTS, mh, ml, 4).then_inc(unit_done, 1)
            pe.wait_ge(lo_done, U_OUT1 + 4)
            row_unit((U_OUT1 + 3) % SLOTS, mh, ml, 6, last=True).then_inc(unit_done, 1)
            ffn(1, U_FFN2, 2, 2, 2)
            mean_squares(3)
            spread(3)

            def attend(k):
                for s in range(SLOTS_A):
                    r, w = divmod(s, 6)
                    q, z, bank = (qa_s if r == 0 else qb_s), kz[r % 2], acc[:, s % 2]
                    if slot_time(s) == k:
                        if w == 0:
                            pe.wait_ge(kz_ready, 3 if r else 1)
                            pe.wait_ge(kz_direct, 2 * r + 2)
                        if s >= 2:
                            pe.wait_ge(logit_out, s - 1)
                        if w < 4:
                            mm = nc.tensor.matmul(bank, q[:, w, P:T], z[:, w // 2], start=True, stop=True)
                        else:
                            for j in (2 * w - 8, 2 * w - 7):
                                mm = nc.tensor.matmul(bank[:, (j % 2) * T:(j % 2 + 1) * T], q[:, j, 0:P],
                                                      z[:, w - 4, :, 0:P], start=True, stop=True)
                        mm.then_inc(score_mm, 1)
                for s in range(SLOTS_A):
                    if slot_time(s) + 1 == k:
                        pe.wait_ge(exp_out, s + 1)
                        if s >= 2:
                            pe.wait_ge(prob_t_out, s - 1)
                        for n in range(4):
                            cols = slice(n * P, (n + 1) * P)
                            mm = nc.tensor.transpose(acc[:, 2 + s % 2, cols], prob[s % 2][:, cols], ident)
                        mm.then_inc(prob_turned, 1)
                for s in range(SLOTS_A):
                    if slot_time(s) + 2 == k:
                        r, w = divmod(s, 6)
                        pe.wait_ge(prob_t_out, s + 1)
                        if r and w in (0, 4):
                            pe.wait_ge(y_taken, 2 * r - (w == 0))
                        nh, h0, b = (2, 2 * w, 1) if w < 4 else (4, 4 * (w - 4), 0)
                        for h in range(nh):
                            head = h0 + h
                            dst = wk[:, 3 - b, head * HD:(head + 1) * HD]
                            g = head // 4
                            for kc in range(b + 1):
                                n = h * (b + 1) + kc
                                mm = nc.tensor.matmul(dst, prob_t[s % 2][:, n * P:(n + 1) * P],
                                                      v2[r % 2][:, kc, g * HD:(g + 1) * HD], start=kc == 0,
                                                      stop=kc == b)
                        mm.then_inc(pv_mm, 1)

            def turn_y(n):
                b = n % 2
                src, bank = ((y_a, acc[:, 2 + b]) if n < 2 else (y_b, acc[:, b]))
                for c in range(4):
                    mm = nc.tensor.transpose(bank[:, c * P:(c + 1) * P], src[:, b, c * P:(c + 1) * P], ident)
                mm.then_inc(y_turned, 1)

            for m in range(20):
                u = U_IN2 + m
                s = u % SLOTS
                pe.wait_ge(lo_done, u + 1)
                if 2 <= m < 14:
                    pe.wait_ge(proj2, m - 1)
                elif m == 14:
                    pe.wait_ge(proj2, 13)
                    pe.wait_ge(blk_lo, 1)
                    nc.tensor.matmul(wk[:, 0, 0:P], zeros[:, 0:P], zeros[:, 0:P], start=True, stop=False,
                                     skip_group_check=True)
                elif m == 18:
                    pe.wait_ge(proj2, 14)
                elif m == 19:
                    pe.wait_ge(hid_taken, 1)
                bank = wk[:, m % 2] if m < 14 else wk[:, 19 - m] if m >= 18 else wk[:, 0]
                for half in range(2):
                    k = position_time(m, half)
                    if k is not None:
                        attend(k)
                    if m in CW:
                        v, j0 = (m - CW[0]) // 2, 8 * (m % 2)
                        dst = bank[:, (2 * v + half) * 32:(2 * v + half + 1) * 32]
                        wh, wl = k_n(w_hi[:, s], 8), k_n(w_lo[:, s], 8)
                        cols = slice(half * P, (half + 1) * P)
                        for j in range(8):
                            bh, bl = (t[:, v, j0 + j] for t in blk_hl)
                            mm = passes(dst, ((wh[:, j, cols], bh), (wh[:, j, cols], bl), (wl[:, j, cols], bh)),
                                        False, j0 == 8 and j == 7)
                    elif m in (2, 6, 7) and half == 1:
                        for tt in range(2):
                            mm = tok_tile(s, tt, bank[:, T + tt * P:T + (tt + 1) * P], slice(P, 2 * P))
                    else:
                        mm = col_tile(s, half, bank[:, half * T:(half + 1) * T],
                                      arrive=(xl_ready, 3 * DC) if (m, half) == (0, 0) else None)
                    if half:
                        mm.then_inc(unit_done, 1)
                    at = (m, half)
                    if at == (0, 0):
                        mean_squares(4)
                    if at == (0, 1):
                        spread(4)
                    if at == (1, 1):
                        pe.wait_ge(rstd_ready, 5)
                        pe.wait_ge(wg_split, 2)
                        for tt in range(2):
                            rows = slice(tt * P, (tt + 1) * P)
                            for c in range(DC):
                                mm = passes(wk[:, 3, tt * 32:tt * 32 + 24],
                                            ((xh[:, c, rows], wg_hi[:, c]), (xh[:, c, rows], wg_lo[:, c]),
                                             (xl[:, c, rows], wg_hi[:, c])), c == 0, c == DC - 1)
                        mm.then_inc(gate_mm, 1)
                    if at == (3, 0):
                        pe.wait_ge(proj2, 3)
                        nc.tensor.matmul(acc[:, 0, 0:T], swap, kf[:, K_A], start=True, stop=True) \
                            .then_inc(key_swapped, 1)
                    if at == (6, 1):
                        pe.wait_ge(proj2, 6)
                        pe.wait_ge(logit_out, 5)
                        nc.tensor.matmul(acc[:, 0], swap, kf[:, K_CK:K_CV + 1], start=True, stop=True) \
                            .then_inc(key_swapped, 1)
                    if at == (8, 0):
                        pe.wait_ge(proj2, 8)
                        pe.wait_ge(blk_ready, 1)
                        pe.wait_ge(logit_out, 6)
                        for n in (K_S, K_W):
                            nc.tensor.matmul(acc[:, n - 1, 0:T], swap, kf[:, n], start=True, stop=True) \
                                .then_inc(key_swapped, 1)
                    if at == (16, 1):
                        pe.wait_ge(prob_t_out, SLOTS_A)
                        pe.wait_ge(y_taken, 2)
                        turn_y(0)
                        turn_y(1)
                    if at == (18, 0):
                        pe.wait_ge(hid_ready, 1)
                        pe.wait_ge(cw2_in, 16 * 3)
                        pe.wait_ge(logit_out, SLOTS_A)
                        for n in range(2):
                            nc.tensor.matmul(acc[:, 0, 0:32], cmp_w2[:, n, 0:P], hid_k[:, n], start=n == 0,
                                             stop=n == 1)
                        for n in range(2):
                            mm = nc.tensor.matmul(acc[:, 1, 0:HD], hv_rep[:, n], cmp_w2[:, n, P:P + HD], start=n == 0,
                                                  stop=n == 1)
                        mm.then_inc(cmp_mm, 1)
                    if at == (18, 1):
                        pe.wait_ge(kcz_ready, 1)
                        pe.wait_ge(y_lo, 2)
                        for b in range(2):
                            for j in range(4):
                                g = j // 2
                                mm = nc.tensor.matmul(acc[:, 2, b * P + 32 * j:b * P + 32 * (j + 1)],
                                                      qb_s[:, j, b * P:(b + 1) * P], kcz[:, :, g * 16:(g + 1) * 16],
                                                      start=True, stop=True)
                        mm.then_inc(cscore_mm, 1)
            pe.wait_ge(cprob, 1)
            for b in range(2):
                mm = nc.tensor.transpose(acc[:, 3, b * P:(b + 1) * P],
                                         prob_c[:, 8 * b:8 * b + 8].rearrange("p h c -> p (h c)"), ident)
            mm.then_inc(cturned, 1)

            def up(m):
                pe.wait_ge(lo_done, U_UP + m + 1)
                for t in range(4):
                    mm = col_tile((U_UP + m) % SLOTS, t, wk[:, 2 * (m % 2) + t // 2, (t % 2) * T:(t % 2 + 1) * T],
                                  4, mh, ml, 4 * (m // 2))
                mm.then_inc(unit_done, 1)

            pe.wait_ge(y_lo, 2)
            pe.wait_ge(proj2, 16)
            up(0)
            pe.wait_ge(cprob_t, 1)
            pe.wait_ge(vblk_ready, 1)
            pe.wait_ge(y_taken, 2 * NBR)
            for b in range(2):
                nc.tensor.matmul(wk[:, 2 + b], prob_ct[:, b], v_blk, start=True, stop=True).then_inc(cout_mm, 1)
            pe.wait_ge(y_taken, 2 * NBR + 2)
            turn_y(2)
            turn_y(3)
            up(1)
            pe.wait_ge(y_lo, 4)
            pe.wait_ge(up_out, 1)
            up(2)
            open_acc()
            pe.wait_ge(up_out, 2)
            up(3)
            for m in range(4):
                if m % 2 == 0:
                    pe.wait_ge(merged_lo, m // 2 + 1)
                pe.wait_ge(lo_done, U_OUT2 + m + 1)
                row_unit((U_OUT2 + m) % SLOTS, xh, xl, 2 * m, last=m == 3).then_inc(unit_done, 1)
            ffn(2, U_FFN3, 5, 4, 5)
            mean_squares(6)
            spread(6)
            for n in range(4):
                pe.wait_ge(x_ready, 7 * DC)
                tt = n // 2
                for c in range(4 * (n % 2), 4 * (n % 2) + 4):
                    pe.wait_ge(y_ready, c + 1)
                    mm = nc.tensor.transpose(acc[:, n, (c % 4) * P:(c % 4 + 1) * P], x[:, c, tt * P:(tt + 1) * P],
                                             ident)
                mm.then_inc(out_turned, 1)



def constants():
    import numpy as np

    f = np.float32
    small = np.zeros((P, C_COLS), f)
    small[:, C_ID:C_ID + P] = np.eye(P)
    small[:, C_SWAP:C_SWAP + P] = np.roll(np.eye(P), 64, axis=0)
    q = np.arange(P)[:, None, None] + P * np.arange(2)[None, :, None]
    valid = (q - (16 * np.arange(NCMP) + 31)[None, None, :]) >= 0
    small[:, C_NEGC:C_NEGC + 30] = np.where(valid, 0, NEG).reshape(P, 30)
    small[:, C_VALC:C_VALC + 30] = valid.reshape(P, 30)
    small[:, C_BLK:C_BLK + 8] = (np.arange(P)[:, None] // 16) == np.arange(8)[None]
    table = np.zeros((P, T_COLS), f)
    inv = (f(1.0) / (f(10000.0) ** (np.arange(0, P, 2, dtype=f) / f(P)))).astype(f)
    ang = (np.arange(T, dtype=f)[None, :] * inv[:, None]).astype(f)
    cos, sin = np.cos(ang), np.sin(ang)
    table[:, T_COS:T_COS + T] = np.concatenate([cos, cos])
    table[:, T_SIN:T_SIN + T] = np.concatenate([-sin, sin])
    keys = np.arange(P)[:, None]
    toks = np.concatenate([np.arange(T), np.arange(P)])[None]
    for h in range(HR):
        lg = np.log1p(-(2.0 ** (-5.0 - h)))
        rel = toks - keys
        table[:, T_DEC + h * DEC:T_DEC + (h + 1) * DEC] = np.where(rel >= 0, np.exp(lg * np.maximum(rel, 0)), 0) \
            * P ** -0.5
    for g, w in enumerate(POOL_WINDOWS):
        table[:, T_RC + g * T:T_RC + (g + 1) * T] = 1.0 / np.minimum(np.arange(1, T + 1), w)
    def bucket(dist):
        dist = np.maximum(dist, 0)
        exact = NBUCKET // 2
        big = exact + (np.log(np.maximum(dist, 1).astype(f) / f(exact)) / f(np.log(128 / exact))
                       * (NBUCKET - exact)).astype(np.int32)
        return np.where(dist < exact, dist, np.minimum(big, NBUCKET - 1))

    dist = np.arange(BIASW) - BIAS_D0
    onehot = (bucket(np.arange(OH_COLS) - OH_D0)[None] == np.arange(NBUCKET)[:, None]).astype(f)
    mask = np.zeros((16, BIASW), f)
    mask[:, dist < 0] = NEG
    mask[0:8, dist >= 128] = NEG
    return {"c_small": small, "c_table": table, "c_onehot": onehot, "c_mask": mask}


def kernel(**inputs):
    import numpy as _np
    import concourse.bacc as _bacc
    from concourse.bass_utils import run_bass_kernel_spmd as _run

    nc = _bacc.Bacc("TRN2", target_bir_lowering=False, num_devices=1)
    arrays, args = {}, {}
    for name, value in {**inputs, **constants()}.items():
        v = _np.ascontiguousarray(value)
        arrays[f"in_{name}"] = v
        args[name] = nc.dram_tensor(f"in_{name}", v.shape, mybir.dt.from_np(v.dtype), kind="ExternalInput").ap()
    out = nc.dram_tensor("out_0", (1, T, D), F32, kind="ExternalOutput").ap()
    build(nc, args, out)
    r = _run(nc, [arrays], core_ids=[0])
    return r.results[0]["out_0"]
```

```python
from contextlib import ExitStack

import concourse.bass as bass
from concourse import mybir

F32 = mybir.dt.float32
F32R = mybir.dt.float32r
BF16 = mybir.dt.bfloat16
I32 = mybir.dt.int32
ALU = mybir.AluOpType
ACT = mybir.ActivationFunctionType
AX_X = mybir.AxisListType.X

P = 128
T = 256
D = 1024
DC = D // P
FF = 2816
EPS = 1e-6
SLOTS = 3
UNIT = 2048
UC = UNIT // DC
FI = FF // UC
NEG = -1e30

HR = 4
POOL_WINDOWS = (2, 4, 8, 16)
PAD = 16
DEC = T + P

HD = 64
NHA = 8
NCMP = 15
NBUCKET = 32
BIASW = 384

OH_D0, OH_COLS = 256, 640
BIAS_D0 = P - 1
NBR = 3
SLOTS_A = 18
GA, GB, CW = (8, 9, 10, 11), (12, 13, 18, 19), (14, 15, 16, 17)

U_FFN1 = 0
U_MIX = U_FFN1 + 3 * FI
U_OUT1 = U_MIX + 10
U_FFN2 = U_OUT1 + 4
U_IN2 = U_FFN2 + 3 * FI
U_UP = U_IN2 + 20
U_OUT2 = U_UP + 4
U_FFN3 = U_OUT2 + 4


def slot_time(s):
    return s if s < 6 else s + 2


def position_time(m, half):
    pos = 2 * m + half
    if 8 <= pos < 16:
        return pos - 8
    return pos - 10 if 18 <= pos < 32 else None


OUT_ORDER = (0, 1, 2, 3)
SUMMED = (0, 1, 2, 4, 5)

V_FFN1, V_MIX, V_FFN2, V_FINAL, V_MIX2, V_FFN3, V_FINAL2 = (8 * n for n in range(7))
V_POOL, V_RET, V_POSK, V_POSV, V_ROWS = 56, 60, 64, 80, 96
V_BOTH, V_COLS = 96, 104

C_ID, C_SWAP, C_NEGC, C_VALC, C_BLK, C_COLS = 0, 128, 256, 286, 316, 324
T_COS, T_SIN, T_DEC, T_RC, T_COLS = 0, 256, 512, 512 + HR * DEC, 512 + HR * DEC + 4 * T


def rows8(v):
    return v.rearrange("(c p) -> c p", p=P)


def bcast(ap, n):
    return ap.unsqueeze(1).to_broadcast([ap.shape[0], n, ap.shape[1]])


def bcast_in(ap, n):
    return ap.unsqueeze(2).to_broadcast([ap.shape[0], ap.shape[1], n])


def build(nc, a, out):
    with ExitStack() as ctx:
        def sb(name, shape, dt=F32):
            return ctx.enter_context(nc.sbuf_tensor(name, shape, dt))

        def sem(name):
            return ctx.enter_context(nc.semaphore(name))

        raw = sb("raw", [P, SLOTS, UNIT])
        w_hi = sb("w_hi", [P, SLOTS, UNIT], F32R)
        w_lo = sb("w_lo", [P, SLOTS, UNIT], F32R)
        x = sb("x", [P, DC, T])
        xh = sb("xh", [P, DC, T], F32R)
        xl = sb("xl", [P, DC, T], F32R)
        mh = sb("mh", [P, DC, T], F32R)
        ml = sb("ml", [P, DC, T], F32R)
        hh = sb("hh", [P, 2, T], F32R)
        hl = sb("hl", [P, 2, T], F32R)
        sq = sb("sq", [P, DC, T])
        work = sb("work", [P, 6, 2 * T])
        arena = sb("arena", [P, 63 * 256])
        cst = sb("cst", [P, C_COLS])
        ones = sb("ones", [P, P])
        mean_d = sb("mean_d", [P, 1])
        mean_h = sb("mean_h", [P, 1])
        zeros = sb("zeros", [P, 512], BF16)
        vec = sb("vec", [P, V_COLS])
        rstd_t = sb("rstd_t", [P, 2])
        rstd_b = sb("rstd_b", [P, T])
        first_r, next_ms = sb("first_r", [P, 2]), sb("next_ms", [P, 2])
        weigh = sb("weigh", [P, DC, 2])
        nr = sb("nr", [P, 3, 8])

        a_s, b_s, t_s, h_s = (work[:, n] for n in range(4))
        diag = work[:, 5, 0:T].rearrange("p (t q) -> p t q", t=2)
        diag_first = work[:, 4, 0:T].rearrange("p (t q) -> p t q", t=2)
        first_b = work[:, 3, 0:T]
        ident = cst[:, C_ID:C_ID + P]
        swap = cst[:, C_SWAP:C_SWAP + P]

        def carve(kib, *shape):
            n = 1
            for s in shape:
                n *= s
            lo = int(kib * 256)
            flat = arena[:, lo:lo + n]
            if len(shape) == 1:
                return flat
            names = " ".join("abcd"[:len(shape)])
            return flat.rearrange(f"p ({names}) -> p {names}", **dict(zip("abcd", shape)))

        x_tok = carve(0, 2, D)
        vec_rows = carve(8, P)

        q_s, k_s = carve(0, HR, T), carve(4, HR, T)
        diag_h = carve(0, 8, P)
        b_h = carve(4, HR, T)
        q_r, k_r = carve(8, HR, T), carve(12, HR, T)
        v_t = carve(16, 2, HR * P)
        pool_u = carve(20, 4, PAD + T)
        win_a, win_b = carve(24.25, 4, PAD + T), carve(28.5, 4, PAD + T)
        o_s = carve(28.5, HR, T)
        st = carve(0, HR, DEC)
        pooled = carve(32.75, 4, T)
        table = carve(36.75, T_COLS)
        pool_ws = carve(48.75, 4, P)
        g_s = work[:, 0:2]
        g_t = work[:, 2:4]
        o_sq = sq[:, 0:HR]

        acc = ctx.enter_context(nc.psum_tensor("acc", [P, 4, 512], F32))
        wk = ctx.enter_context(nc.psum_tensor("wk", [P, 4, 512], F32))

        oh = carve(51, OH_COLS)[0:NBUCKET]
        bias_mask = carve(54.5, BIASW)[0:16]
        bias_rows = carve(56, BIASW)[0:16]
        bias_table = carve(57.5, 16)[0:NBUCKET]
        conv_rows = carve(58, 4, P)[0:44]
        bias_c = carve(62, 2, NHA, NCMP)
        bias = carve(0, 16, T)
        ga, gb = carve(16, DC, T), carve(24, DC, T)
        blk = carve(24, 2, 16, 32)
        kz = [carve(32 + 4 * n, 2, 2, T) for n in range(2)]
        qa_s, qb_s = carve(40, 4, T), carve(44, 4, T)
        logit = [carve(48 + 2 * n, 512) for n in range(2)]
        prob = [carve(52 + 2 * n, 512) for n in range(2)]
        prob_t = [carve(56 + 2 * n, 512) for n in range(2)]
        v2 = [carve(60 + n, 2, P) for n in range(2)]
        v_blk = carve(48, 8, HD)
        hid_rows = carve(50, 512)[0:32]
        prob_ct = carve(52, 2, P)
        sqf = sq[:].rearrange("p c t -> p (c t)")
        kf = sqf[:, 0:5 * T].rearrange("p (n t) -> p n t", n=5)
        K_A, K_S, K_W, K_CK, K_CV = range(5)
        cmp_w2 = sqf[:, 0:384].rearrange("p (n d) -> p n d", n=2)
        hv_rep = sqf[:, 2 * T:3 * T].rearrange("p (n m) -> p n m", n=2)
        prob_c = sqf[:, 1280:1536].rearrange("p (m c) -> p m c", c=16)
        hid_x, hid_z, hid_t = (sqf[:, 1536 + n * P:1536 + (n + 1) * P] for n in range(3))
        hid_k = sqf[:, 1920:1984].rearrange("p (n m) -> p n m", n=2)
        kcz = sqf[:, 1984:2048].rearrange("p (h m) -> p h m", h=2)
        y_a, y_b, y_tmp = work[:, 0:2], work[:, 2:4], work[:, 4]
        wg_raw = work[:, 5, T:T + 192].rearrange("p (k n) -> p k n", k=DC)
        wg_hi, wg_lo = sb("wg_hi", [P, DC, 24], F32R), sb("wg_lo", [P, DC, 24], F32R)
        conv = sb("conv", [P, 4, 44])
        sink = sb("sink", [P, NHA])
        gates = sb("gates", [P, 2, 24])
        half_r = sb("half_r", [P, 2])
        mx, nmx, sums = (sb(n, [P, NBR, 2, NHA]) for n in ("mx", "nmx", "sums"))
        coef = sb("coef", [P, 2, NHA])
        mx_c, sum_c = sb("mx_c", [P, 16]), sb("sum_c", [P, 16])
        blk_hl = [t[:, 4:8].rearrange("p a b -> p (a b)").rearrange("p (v j m) -> p v j m", v=2, j=16)
                  for t in (mh, ml)]
        conv_a, conv_b, t3_s, h3_s = (work[:, n] for n in range(2, 6))
        out_s = carve(0, 2, D)
        y_f = carve(16, DC, T)
        out_banks = [wk[:, 0], wk[:, 1], wk[:, 2], acc[:, 0]]
        scratch = nc.dram_tensor("bias_scratch", (16, BIASW), F32, kind="Internal").ap()

        def acc_tile(n):
            return acc[:, n // 2, (n % 2) * T:(n % 2 + 1) * T]

        def halves(bank):
            return bank.rearrange("p (h t) -> p h t", t=T)

        raw_in = [sem(f"raw_in{s}") for s in range(SLOTS)]
        hi_done, lo_done, unit_done = sem("hi_done"), sem("lo_done"), sem("unit_done")
        table_in, pw_in = sem("table_in"), sem("pw_in")
        ident_in, gain_in, small_in, vec_in = (sem(n) for n in ("ident_in", "gain_in", "small_in", "vec_in"))
        x_in = [sem(f"x_in{n}") for n in range(2)]
        gain_turned, gain_ready, bias_cmp_out = sem("gain_turned"), sem("gain_ready"), sem("bias_cmp_out")
        const_set = sem("const_set")
        vec_turned, vec_ready = sem("vec_turned"), sem("vec_ready")
        acc_ready, x_ready, xh_ready, xl_ready, sq_ready = (
            sem(n) for n in ("acc_ready", "x_ready", "xh_ready", "xl_ready", "sq_ready"))
        ms_ready, diag_ready, spread_ready, rstd_ready = (
            sem(n) for n in ("ms_ready", "diag_ready", "spread_ready", "rstd_ready"))
        dve_step = sem("dve_step")
        a_out, tanh_out, b_out, h1_out, h_out, hh_out, hl_out = (
            sem(n) for n in ("a_out", "tanh_out", "b_out", "h1_out", "h_out", "hh_out", "hl_out"))
        proj_out = sem("proj_out")
        swapped, rope_cos, rope_out = sem("swapped"), sem("rope_cos"), sem("rope_out")
        pool_win, pooled_out, pool_mm, pool_hi, pool_lo = (
            sem(n) for n in ("pool_win", "pooled_out", "pool_mm", "pool_hi", "pool_lo"))
        pool_step = sem("pool_step")
        st_mm, st_out, o_mm, o_out, osq_out = (sem(n) for n in ("st_mm", "st_out", "o_mm", "o_out", "osq_out"))
        hms_ready, hdiag_ready, hspread_ready = (sem(n) for n in ("hms_ready", "hdiag_ready", "hspread_ready"))
        gate_tanh, head_out, head_hi, head_lo = (
            sem(n) for n in ("gate_tanh", "head_out", "head_hi", "head_lo"))
        bias_in, conv_in, cw2_in, wg_in, sink_in = (
            sem(n) for n in ("bias_in", "conv_in", "cw2_in", "wg_in", "sink_in"))
        bias_mm, bias_cmp_mm, bias_row, bias_written, bias_ready = (
            sem(n) for n in ("bias_mm", "bias_cmp_mm", "bias_row", "bias_written", "bias_ready"))
        y_ready, wg_split, gate_mm, gate_raw, half_ready = (
            sem(n) for n in ("y_ready", "wg_split", "gate_mm", "gate_raw", "half_ready"))
        proj2, key_swapped, kz_zero, kz_direct, kz_ready = (
            sem(n) for n in ("proj2", "key_swapped", "kz_zero", "kz_direct", "kz_ready"))
        ga_tanh = sem("ga_tanh")
        score_mm, logit_out, neg_max, exp_out, prob_turned, prob_t_out, pv_mm, y_taken = (
            sem(n) for n in ("score_mm", "logit_out", "neg_max", "exp_out", "prob_turned", "prob_t_out", "pv_mm",
                             "y_taken"))
        sink_gap, sink_exp = sem("sink_gap"), sem("sink_exp")
        blk_zero, blk_ready, blk_hi, blk_lo = (sem(n) for n in ("blk_zero", "blk_ready", "blk_hi", "blk_lo"))
        hid_rows_out, hid_turned = sem("hid_rows_out"), sem("hid_turned")
        hid_z_ready, hid_tanh, hid_ready, hid_taken = (
            sem(n) for n in ("hid_z_ready", "hid_tanh", "hid_ready", "hid_taken"))
        cmp_mm, kcz_ready, vblk_ready, cscore_mm, clogit, cexp, cprob, cturned, cprob_t, cout_mm = (
            sem(n) for n in ("cmp_mm", "kcz_ready", "vblk_ready", "cscore_mm", "clogit", "cexp", "cprob",
                             "cturned", "cprob_t", "cout_mm"))
        y_turned, y_hi, y_lo = (sem(n) for n in ("y_turned", "y_hi", "y_lo"))
        up_out, merged, merged_hi, merged_lo = (sem(n) for n in ("up_out", "merged", "merged_hi", "merged_lo"))
        conv_0, conv_1, conv_2 = sem("conv_0"), sem("conv_1"), sem("conv_2")
        out_turned, out_copied, out_copied_act = sem("out_turned"), sem("out_copied"), sem("out_copied_act")
        sq_added, weigh_ready, first_diag, first_spread = (
            sem(n) for n in ("sq_added", "weigh_ready", "first_diag", "first_spread"))
        out_written = sem("out_written")

        def raw_count(u):
            return 16 * (u // SLOTS + 1)

        w_rows = lambda w, r0: w[r0:r0 + 2 * P, :].rearrange("(k p) n -> p k n", p=P)

        def w_cols(w):
            return w.rearrange("(k p) n -> p k n", p=P)

        def k_n(tile, k):
            return tile.rearrange("p (k n) -> p k n", k=k)

        block = ctx.enter_context(nc.Block())

        @block.sync
        def _(sp):

            def unit(u, src, k, slot=None, count=None):
                slot = u % SLOTS if slot is None else slot
                if count is None:
                    count = u - 2
                if not isinstance(count, int) or count > 0:
                    sp.wait_ge(lo_done, count)
                sp.dma_start(k_n(raw[:, slot], k), src).then_inc(raw_in[slot], 16)

            def small_loads():
                sp.dma_start(cst[:, P:], a["c_small"][:, P:]).then_inc(small_in, 16)
                for col, name in ((V_MIX, "mix_norm"), (V_FFN2, "ffn2_norm"), (V_MIX2, "norm_mix_2"),
                                  (V_FFN3, "norm_ffn_2"), (V_POOL, "pool_scale"), (V_RET, "ret_norm")):
                    v = rows8(a[name][0])
                    sp.dma_start(vec_rows[col:col + v.shape[0], :], v).then_inc(vec_in, 16)
                for col, name in ((V_FINAL, "final_norm"), (V_FINAL2, "norm_final_2")):
                    sp.dma_start(vec_rows[col:col + DC, :], rows8(a[name])).then_inc(vec_in, 16)
                for col, name in ((V_POSK, "cmp_pos_k_2"), (V_POSV, "cmp_pos_v_2")):
                    sp.dma_start(vec_rows[col:col + 16, :],
                                 a[name][0].rearrange("(j s) d -> j (s d)", s=2)).then_inc(vec_in, 16)
                for j in range(3):
                    sp.dma_start(conv_rows[:, j], rows8(a["conv_w_2"][0, j])).then_inc(conv_in, 16)
                sp.dma_start(conv_rows[:, 3], rows8(a["conv_b_2"][0])).then_inc(conv_in, 16)
                sp.dma_start(sink[:], a["attn_sinks_2"][0].partition_broadcast(P)).then_inc(sink_in, 16)
                sp.dma_start(wg_raw, w_cols(a["w_in_2"][0])[:, :, 2048:2072]).then_inc(wg_in, 16)

            def ffn(base, w1, off1, w3, off3, w2):
                c1, c3 = w_cols(w1)[:, :, off1:off1 + FF], w_cols(w3)[:, :, off3:off3 + FF]
                r2 = w2.rearrange("(k p) n -> p k n", p=P)
                unit(base, c1[:, :, 0:UC], DC)
                unit(base + 1, c3[:, :, 0:UC], DC)
                unit(base + 2, c1[:, :, UC:2 * UC], DC)
                if base == U_FFN1:
                    small_loads()
                unit(base + 3, c3[:, :, UC:2 * UC], DC)
                unit(base + 4, r2[:, 0:2, :], 2)
                c1, c3 = c1[:, :, UC:], c3[:, :, UC:]
                with sp.Fori(2, FI) as i:
                    unit(None, c1[:, :, bass.ds((i - 1) * UC, UC)], DC, (base + 2) % SLOTS, i * 3 + (base - 3))
                    unit(None, c3[:, :, bass.ds((i - 1) * UC, UC)], DC, base % SLOTS, i * 3 + (base - 2))
                    unit(None, r2[:, bass.ds(i * 2 - 2, 2), :], 2, (base + 1) % SLOTS, i * 3 + (base - 1))
                unit(base + 3 * FI - 1, r2[:, 2 * FI - 2:2 * FI, :], 2)

            sp.dma_start(cst[:, 0:P], a["c_small"][:, 0:P]).then_inc(ident_in, 16)
            for n in range(2):
                cols = slice(n * D // 2, (n + 1) * D // 2)
                sp.dma_start(x_tok[:, :, cols], a["x"][0].rearrange("(t p) n -> p t n", p=P)[:, :, cols]) \
                    .then_inc(x_in[n], 16)
            ffn(U_FFN1, a["ffn1_w1"][0], 0, a["ffn1_w3"][0], 0, a["ffn1_w2"][0])
            w_in = w_cols(a["w_in"][0])
            for m, c in enumerate((2, 3, 4, 5, 0, 1, 6, 7, 8, 9)):
                unit(U_MIX + m, w_in[:, :, c * UC:(c + 1) * UC], DC)
            for m in range(4):
                unit(U_OUT1 + m, w_rows(a["w_out"][0], 2 * P * m), 2)
            ffn(U_FFN2, a["ffn2_w1"][0], 0, a["ffn2_w3"][0], 0, a["ffn2_w2"][0])
            w2 = w_cols(a["w_in_2"][0])
            for m in range(20):
                if m in CW:
                    src = a["cmp_w1_k_2" if m < CW[2] else "cmp_w1_v_2"][0]
                    src = src.rearrange("(j p) n -> p j n", p=P)[:, 8 * (m % 2):8 * (m % 2) + 8]
                else:
                    c0 = m * UC if m < 8 else 2072 + (m - 8) * UC if m < 14 else 3096 + (m - 16) * UC
                    src = w2[:, :, c0:c0 + UC]
                unit(U_IN2 + m, src, DC)
            for m in range(4):
                src = w_cols(a["w_up_a_2" if m < 2 else "w_up_b_2"][0])
                unit(U_UP + m, src[:, :, (m % 2) * 512:(m % 2 + 1) * 512], 4)
            for m in range(4):
                unit(U_OUT2 + m, w_rows(a["w_out_2"][0], 2 * P * m), 2)
            wf = a["w_ffn_in_2"][0]
            ffn(U_FFN3, wf, FF, wf, 0, a["w_ffn_out_2"][0])
            for n in range(4):
                half, tt = divmod(OUT_ORDER[n], 2)
                sp.wait_ge(out_copied_act if n % 2 else out_copied, n // 2 + 1)
                sp.dma_start(out[0, tt * P:(tt + 1) * P, half * 512:(half + 1) * 512],
                             out_s[:, tt, half * 512:(half + 1) * 512]).then_inc(out_written, 16)
            sp.wait_ge(out_written, 64)

        @block.scalar
        def _(act):
            act.dma_start(vec_rows[V_FFN1:V_FFN1 + DC, :], rows8(a["ffn1_norm"][0])).then_inc(gain_in, 16)
            act.dma_start(oh, a["c_onehot"]).then_inc(bias_in, 16)
            act.dma_start(bias_table, a["rel_bias_table_2"]).then_inc(bias_in, 16)
            act.dma_start(bias_mask, a["c_mask"]).then_inc(bias_in, 16)

            def hi(u):
                act.wait_ge(raw_in[u % SLOTS], raw_count(u))
                if u >= SLOTS:
                    act.wait_ge(unit_done, u - 2)
                nc.scalar.activation(w_hi[:, u % SLOTS], raw[:, u % SLOTS], ACT.Copy).then_inc(hi_done, 1)

            def hi_in_loop(i, base, c):
                s = (base + c) % SLOTS
                act.wait_ge(raw_in[s], i * 16 + 16 * ((base + c) // SLOTS + 1))
                act.wait_ge(unit_done, i * 3 + (base + c - 2))
                nc.scalar.activation(w_hi[:, s], raw[:, s], ACT.Copy).then_inc(hi_done, 1)

            def handoff(n, gain):
                for c in range(DC + 1):
                    if c < DC:
                        act.wait_ge(x_ready, DC * n + c + 1)
                        nc.scalar.activation(xh[:, c], x[:, c], ACT.Copy, scale=vec[:, gain + c:gain + c + 1]) \
                            .then_inc(xh_ready, 1)
                    if c:
                        nc.scalar.activation(sq[:, c - 1], x[:, c - 1], ACT.Square).then_inc(sq_ready, 1)

            def ffn(f, base):
                n0 = FI * f

                def tanh(i):
                    act.wait_ge(a_out, i + (n0 + 1))
                    nc.scalar.activation(t_s, a_s, ACT.Tanh, scale=0.5).then_inc(tanh_out, 1)

                def h_hi(i, w2_before):
                    act.wait_ge(h_out, i + (n0 + 1))
                    if w2_before is not None:
                        act.wait_ge(unit_done, w2_before)
                    nc.scalar.activation(hh[:].rearrange("p a t -> p (a t)"), h_s, ACT.Copy).then_inc(hh_out, 1)

                hi(base + 2)
                tanh(0)
                hi(base + 3)
                h_hi(0, None)
                with act.Fori(1, FI) as i:
                    hi_in_loop(i, base, 1)
                    tanh(i)
                    hi_in_loop(i, base, 2)
                    hi_in_loop(i, base, 3)
                    h_hi(i, i * 3 + (base + 2))
                hi(base + 3 * FI + 1)

            act.wait_ge(gain_ready, 1)
            hi(0)
            handoff(0, V_FFN1)
            hi(1)
            act.wait_ge(bias_row, 1)
            act.dma_start(scratch, bias_rows).then_inc(bias_written, 16)
            act.dma_start(table, a["c_table"]).then_inc(table_in, 16)
            act.dma_start(pool_ws, a["pool_w"][0].rearrange("g k n -> k g n")).then_inc(pw_in, 16)
            ffn(0, U_FFN1)
            handoff(1, V_MIX)
            def o_copy(j):
                act.wait_ge(o_mm, j + 1)
                nc.scalar.activation(o_s[:, 2 * j:2 * j + 2], halves(wk[:, 2 + j]), ACT.Copy).then_inc(o_out, 1)

            def pool_hi_part(j):
                for g in (2 * j, 2 * j + 1):
                    act.wait_ge(pool_mm, 2)
                    nc.scalar.activation(mh[:, g], acc[:, j, (g % 2) * T:(g % 2 + 1) * T], ACT.Copy,
                                         scale=vec[:, V_POOL + g:V_POOL + g + 1]).then_inc(pool_hi, 1)

            def gate(j):
                act.wait_ge(proj_out, 9 + j)
                nc.scalar.activation(g_t[:, j], g_s[:, j], ACT.Tanh, scale=0.5).then_inc(gate_tanh, 1)

            for m in range(10):
                hi(U_MIX + m + 2)
                if m == 8:
                    act.wait_ge(pooled_out, 1)
                    o_copy(0)
                    o_copy(1)
                if m == 9:
                    pool_hi_part(0)
                    pool_hi_part(1)
                    gate(0)
            gate(1)
            hi(U_OUT1 + 2)
            hi(U_OUT1 + 3)
            for j in range(2):
                act.wait_ge(head_out, j + 1)
                nc.scalar.activation(mh[:, 4 + 2 * j:6 + 2 * j], b_h[:, 2 * j:2 * j + 2], ACT.Copy) \
                    .then_inc(head_hi, 1)
            hi(U_OUT1 + 4)
            hi(U_OUT1 + 5)
            handoff(2, V_FFN2)
            ffn(1, U_FFN2)
            act.wait_ge(weigh_ready, 2)
            handoff(3, V_BOTH)
            act.wait_ge(wg_in, 16)
            nc.scalar.activation(wg_hi[:], wg_raw, ACT.Copy).then_inc(wg_split, 1)

            def attend(k):
                for s in range(SLOTS_A):
                    if slot_time(s) + 1 == k:
                        act.wait_ge(prob_turned, s + 1)
                        if s >= 2:
                            act.wait_ge(pv_mm, s - 1)
                        nc.scalar.activation(prob_t[s % 2], acc[:, 2 + s % 2], ACT.Copy).then_inc(prob_t_out, 1)
                for s in range(SLOTS_A):
                    if slot_time(s) == k:
                        r, w = divmod(s, 6)
                        nh, h0, b = (2, 2 * w, 1) if w < 4 else (4, 4 * (w - 4), 0)
                        act.wait_ge(neg_max, s + 1)
                        if s >= 2:
                            act.wait_ge(prob_turned, s - 1)
                        n = 512 // nh
                        for h in range(nh):
                            cols = slice(h * n, (h + 1) * n)
                            ex = nc.scalar.activation(prob[s % 2][:, cols], logit[s % 2][:, cols], ACT.Exp,
                                                      bias=nmx[:, r, b, h0 + h:h0 + h + 1],
                                                      accum_out=sums[:, r, b, h0 + h:h0 + h + 1])
                        ex.then_inc(exp_out, 1)

            def key_halves(n):
                act.wait_ge(key_swapped, (1, 3, 4)[n])
                act.wait_ge(kz_zero, 2)
                if n == 2:
                    act.wait_ge(score_mm, 6)
                z, bank = kz[n % 2], acc[:, (0, 0, 1)[n]]
                nc.scalar.activation(z[0:HD, 1, 0], bank[0:HD, 0:T], ACT.Copy)
                nc.scalar.activation(z[HD:P, 0, 1], bank[HD:P, 0:T], ACT.Copy).then_inc(kz_ready, 1)

            def y_hi_part(n):
                act.wait_ge(y_turned, n + 1)
                c0, b = 4 * (n // 2), n % 2
                bank = acc[:, 2 + b] if n < 2 else acc[:, b]
                nc.scalar.activation(mh[:, c0:c0 + 4, b * P:(b + 1) * P], k_n(bank, 4), ACT.Copy).then_inc(y_hi, 1)

            def gate_tanhs(j, n_out):
                act.wait_ge(proj2, n_out)
                buf = (ga if j < 4 else gb)[:, 2 * (j % 4):2 * (j % 4) + 2]
                nc.scalar.activation(buf, buf, ACT.Tanh, scale=0.5).then_inc(ga_tanh, 1)

            for m in range(20):
                if m == 2:
                    act.wait_ge(gate_mm, 1)
                    act.wait_ge(half_ready, 1)
                    for tt in range(2):
                        g = nc.scalar.activation(gates[:, tt], acc[:, 0, tt * 32:tt * 32 + 24], ACT.Tanh,
                                                 scale=half_r[:, tt:tt + 1])
                    g.then_inc(gate_raw, 1)
                for half in range(2):
                    k = position_time(m, half)
                    if k is not None:
                        attend(k)
                    if (m, half) == (19, 0):
                        act.wait_ge(hid_z_ready, 1)
                        nc.scalar.activation(hid_t, hid_z, ACT.Tanh, scale=0.7978845608028654).then_inc(hid_tanh, 1)
                    if half == 0:
                        hi(U_IN2 + m + 2)
                    if (m, half) == (3, 1):
                        key_halves(0)
                    if (m, half) == (7, 1):
                        act.wait_ge(blk_ready, 1)
                        nc.scalar.activation(blk_hl[0], blk, ACT.Copy).then_inc(blk_hi, 1)
                    if (m, half) == (8, 0):
                        key_halves(1)
                        key_halves(2)
                    if half == 1 and 9 <= m < 15:
                        gate_tanhs(m - 9, m)
                    if (m, half) == (17, 0):
                        y_hi_part(0)
                        y_hi_part(1)
                    if k == 7:
                        act.wait_ge(sink_gap, 1)
                        nc.scalar.activation(mx[:, 0], mx[:, 0], ACT.Exp).then_inc(sink_exp, 1)
            hi_next = U_UP + 2
            gate_tanhs(6, 15)
            act.wait_ge(cmp_mm, 1)
            act.wait_ge(kz_zero, 3)
            nc.scalar.activation(kcz[0:HD, 0], acc[0:HD, 0, 0:32], ACT.Copy)
            nc.scalar.activation(kcz[HD:P, 1], acc[HD:P, 0, 0:32], ACT.Copy).then_inc(kcz_ready, 1)
            act.wait_ge(clogit, 1)
            nc.scalar.activation(prob_c[:, :, 0:NCMP], prob_c[:, :, 0:NCMP], ACT.Exp).then_inc(cexp, 1)
            gate_tanhs(7, 16)
            hi(hi_next)
            act.wait_ge(cturned, 1)
            nc.scalar.activation(prob_ct, k_n(acc[:, 3, 0:T], 2), ACT.Copy).then_inc(cprob_t, 1)
            hi(hi_next + 1)
            y_hi_part(2)
            y_hi_part(3)
            hi(hi_next + 2)
            for j in range(2):
                if j:
                    hi(hi_next + 3)
                act.wait_ge(merged, j + 1)
                nc.scalar.activation(xh[:, 4 * j:4 * j + 4], ga[:, 4 * j:4 * j + 4], ACT.Copy).then_inc(merged_hi, 1)
            for u in range(U_OUT2 + 2, U_OUT2 + 6):
                hi(u)
            handoff(4, V_FFN3)

            def conv_start(i, n, src, dst, f0, out_sem):
                act.wait_ge(out_sem, i + (2 * FI + 1))
                for t in range(2):
                    f = f0 + t + i * 2
                    nc.scalar.activation(k_n(dst, 2)[:, t], k_n(src, 2)[:, t], ACT.Identity,
                                         scale=conv[:, 2, bass.ds(f, 1)], bias=conv[:, 3, bass.ds(f, 1)]) \
                        .then_inc(conv_0, 1)

            def ffn3_step(i, last):
                n0 = 2 * FI
                if i is not None and not (isinstance(i, int) and i == 0):
                    hi_in_loop(i, U_FFN3, 1)
                else:
                    hi(U_FFN3 + 2)
                if isinstance(i, int) and i == 0:
                    hi(U_FFN3 + 3)
                else:
                    hi_in_loop(i, U_FFN3, 2)
                conv_start(i, 0, a_s, conv_a, 22, a_out)
                act.wait_ge(conv_2, i * 4 + 2)
                nc.scalar.activation(t3_s, conv_a, ACT.Tanh, scale=0.5).then_inc(tanh_out, 1)
                conv_start(i, 1, b_s, conv_b, 0, b_out)
                if not (isinstance(i, int) and i == 0) and not last:
                    hi_in_loop(i, U_FFN3, 3)
                act.wait_ge(h_out, i + (n0 + 1))
                if not (isinstance(i, int) and i == 0):
                    act.wait_ge(unit_done, i * 3 + (U_FFN3 + 2))
                nc.scalar.activation(hh[:].rearrange("p a t -> p (a t)"), h3_s, ACT.Copy).then_inc(hh_out, 1)

            ffn3_step(0, False)
            with act.Fori(1, FI - 1) as i:
                ffn3_step(i, False)
            ffn3_step(FI - 1, True)
            for c in range(DC):
                act.wait_ge(x_ready, 5 * DC + c + 1)
                nc.scalar.activation(y_f[:, c], x[:, c], ACT.Copy, scale=vec[:, V_FINAL2 + c:V_FINAL2 + c + 1]) \
                    .then_inc(y_ready, 1)
                nc.scalar.activation(sq[:, c], x[:, c], ACT.Square).then_inc(sq_ready, 1)
            act.wait_ge(rstd_ready, 6)
            for n in (1, 3):
                half, tt = divmod(OUT_ORDER[n], 2)
                act.wait_ge(out_turned, n + 1)
                nc.scalar.activation(out_s[:, tt, half * 512:(half + 1) * 512], out_banks[n], ACT.Copy,
                                     scale=rstd_t[:, tt:tt + 1]).then_inc(out_copied_act, 1)

        @block.gpsimd
        def _(pool):
            nc.gpsimd.memset(ones[:], 1.0).then_inc(const_set, 1)
            nc.gpsimd.memset(mean_d[:], 1.0 / D).then_inc(const_set, 1)
            nc.gpsimd.memset(mean_h[:], 1.0 / P).then_inc(const_set, 1)
            nc.gpsimd.memset(zeros[:], 0.0).then_inc(const_set, 1)

            def add_squares(k):
                for c in range(1, DC):
                    pool.wait_ge(sq_ready, DC * SUMMED[k] + c + 1)
                    if c > 1:
                        pool.wait_ge(sq_added, (DC - 1) * k + c - 1)
                    nc.gpsimd.tensor_tensor(sq[:, c], sq[:, c], sq[:, c - 1], ALU.add).then_inc(sq_added, 1)

            add_squares(0)
            add_squares(1)
            steps = [0]

            def step(ins):
                ins.then_inc(pool_step, 1)
                steps[0] += 1
                pool.wait_ge(pool_step, steps[0])

            for buf in (pool_u, win_a, win_b):
                nc.gpsimd.memset(buf[:, :, 0:PAD], 0.0).then_inc(pool_step, 1)
                steps[0] += 1
            pool.wait_ge(pool_step, steps[0])
            pool.wait_ge(table_in, 16)
            for j, (src, dst) in enumerate(((q_s, q_r), (q_s, q_r), (k_s, k_r), (k_s, k_r))):
                pool.wait_ge(proj_out, 1 + j)
                h = 2 * (j % 2)
                nc.gpsimd.tensor_tensor(dst[:, h:h + 2], src[:, h:h + 2], bcast(table[:, T_COS:T_COS + T], 2),
                                        ALU.mult).then_inc(rope_cos, 1)
            pool.wait_ge(proj_out, 6)
            for g0, by, src, dst in ((0, 1, pool_u, win_a), (1, 2, win_a, win_b), (2, 4, win_b, win_a),
                                     (3, 8, win_a, win_b)):
                last = nc.gpsimd.tensor_tensor(dst[:, g0:, by:], src[:, g0:, by:], src[:, g0:, 0:PAD + T - by],
                                               ALU.add)
                if g0 < 3:
                    step(last)
                else:
                    last.then_inc(pool_win, 1)
            for j in range(2):
                pool.wait_ge(o_out, j + 1)
                nc.gpsimd.tensor_tensor(o_sq[:, 2 * j:2 * j + 2], o_s[:, 2 * j:2 * j + 2],
                                        o_s[:, 2 * j:2 * j + 2], ALU.mult).then_inc(osq_out, 1)
            add_squares(2)
            pool.wait_ge(bias_written, 16)
            nc.gpsimd.dma_start(bias, bass.AP(tensor=scratch.tensor, offset=0,
                                              ap=[[1, P], [BIASW, 16], [1, T]])).then_inc(bias_ready, 16)
            for z in kz:
                nc.gpsimd.memset(z, 0.0).then_inc(kz_zero, 1)
            nc.gpsimd.memset(blk, 0.0).then_inc(blk_zero, 1)

            def key_direct(n, n_out):
                pool.wait_ge(proj2, n_out)
                if n == 2:
                    pool.wait_ge(score_mm, 6)
                pool.wait_ge(kz_zero, 2)
                nc.gpsimd.tensor_copy(kz[n % 2][0:HD, 0, 0], kf[0:HD, n]).then_inc(kz_direct, 1)
                pool.wait_ge(kz_direct, 2 * n + 1)
                nc.gpsimd.tensor_copy(kz[n % 2][HD:P, 1, 1], kf[HD:P, n]).then_inc(kz_direct, 1)
                pool.wait_ge(kz_direct, 2 * n + 2)

            key_direct(0, 3)
            key_direct(1, 7)
            key_direct(2, 8)
            nc.gpsimd.memset(kcz, 0.0).then_inc(kz_zero, 1)
            nc.gpsimd.memset(prob_c, 0.0).then_inc(kz_zero, 1)
            pool.wait_ge(key_swapped, 4)
            pool.wait_ge(kz_direct, 6)
            for c0, name in ((0, "cmp_w2_k_2"), (HD, "cmp_w2_k_2"), (2 * HD, "cmp_w2_v_2")):
                nc.gpsimd.dma_start(cmp_w2[:, :, c0:c0 + HD], w_cols(a[name][0])).then_inc(cw2_in, 16)
            add_squares(3)
            add_squares(4)

        @block.vector
        def _(dve):
            steps = [0]

            def step(ins):
                ins.then_inc(dve_step, 1)
                steps[0] += 1
                dve.wait_ge(dve_step, steps[0])

            def lo(u):
                dve.wait_ge(hi_done, u + 1)
                s = u % SLOTS
                nc.vector.tensor_tensor(w_lo[:, s], raw[:, s], w_hi[:, s].bitcast(F32), ALU.subtract) \
                    .then_inc(lo_done, 1)

            def lo_in_loop(i, base, c):
                s = (base + c) % SLOTS
                dve.wait_ge(hi_done, i * 3 + (base + c + 1))
                nc.vector.tensor_tensor(w_lo[:, s], raw[:, s], w_hi[:, s].bitcast(F32), ALU.subtract) \
                    .then_inc(lo_done, 1)

            def x_lo(c, n, gain):
                dve.wait_ge(xh_ready, DC * n + c + 1)
                nc.vector.scalar_tensor_tensor(out=xl[:, c], in0=x[:, c], scalar=vec[:, gain + c:gain + c + 1],
                                               in1=xh[:, c].bitcast(F32), op0=ALU.mult, op1=ALU.subtract) \
                    .then_inc(xl_ready, 1)

            def add_residual(c, na, coef):
                dve.wait_ge(acc_ready, DC * na + c // 2 * 2 + 2)
                if coef is None:
                    nc.vector.tensor_copy(x[:, c], acc_tile(c)).then_inc(x_ready, 1)
                else:
                    nc.vector.scalar_tensor_tensor(out=x[:, c], in0=acc_tile(c), scalar=coef, in1=x[:, c],
                                                   op0=ALU.mult, op1=ALU.add).then_inc(x_ready, 1)

            def handoff(n, coef, gain):
                for c in range(DC + 1):
                    if c < DC:
                        add_residual(c, n, coef)
                    if c:
                        x_lo(c - 1, n, gain)

            def rsqrt(src, n):
                v, r, t = (nr[:, j, 0:n] for j in range(3))
                step(nc.vector.tensor_scalar(v, src, EPS, None, ALU.add))
                step(nc.vector.tensor_scalar(r.bitcast(I32), v.bitcast(I32), 1, None, ALU.logical_shift_right))
                step(nc.vector.tensor_scalar(r.bitcast(I32), r.bitcast(I32), -1.0, float(0x5F3759DF),
                                             ALU.mult, ALU.add))
                for _ in range(4):
                    step(nc.vector.scalar_tensor_tensor(out=t, in0=r, scalar=-0.5, in1=r, op0=ALU.mult, op1=ALU.mult))
                    step(nc.vector.tensor_tensor(t, t, v, ALU.mult))
                    step(nc.vector.scalar_tensor_tensor(out=r, in0=t, scalar=1.5, in1=r, op0=ALU.add, op1=ALU.mult))
                return r

            def rstd(n):
                dve.wait_ge(ms_ready, n + 1)
                r = rsqrt(wk[:, 3, 0:2], 2)
                step(nc.vector.tensor_copy(rstd_t[:], r))
                for tt in range(2):
                    nc.vector.tensor_scalar(diag[:, tt], ident, rstd_t[:, tt:tt + 1], None, ALU.mult) \
                        .then_inc(diag_ready, 1)
                dve.wait_ge(spread_ready, n + 1)
                nc.vector.tensor_copy(rstd_b[:], wk[:, 3, T:2 * T]).then_inc(rstd_ready, 1)
                dve.wait_ge(rstd_ready, n + 1)

            def rstd_both():
                dve.wait_ge(ms_ready, 4)
                ms = wk[:, 3, 0:4].rearrange("p (t n) -> p n t", n=2)
                r = rsqrt(ms[:, 0], 2)
                step(nc.vector.tensor_copy(first_r[:], r))
                step(nc.vector.tensor_tensor(next_ms[:], first_r[:], first_r[:], ALU.mult))
                step(nc.vector.tensor_tensor(next_ms[:], next_ms[:], ms[:, 1], ALU.mult))
                r = rsqrt(next_ms[:], 2)
                step(nc.vector.tensor_tensor(rstd_t[:], first_r[:], r, ALU.mult))
                for tt in range(2):
                    nc.vector.tensor_scalar(diag[:, tt], ident, rstd_t[:, tt:tt + 1], None, ALU.mult) \
                        .then_inc(diag_ready, 1)
                for tt in range(2):
                    nc.vector.tensor_scalar(diag_first[:, tt], ident, first_r[:, tt:tt + 1], None, ALU.mult) \
                        .then_inc(first_diag, 1)
                dve.wait_ge(spread_ready, 4)
                nc.vector.tensor_copy(rstd_b[:], wk[:, 3, T:2 * T]).then_inc(rstd_ready, 1)
                dve.wait_ge(rstd_ready, 4)
                dve.wait_ge(first_spread, 1)
                step(nc.vector.tensor_copy(first_b, wk[:, 2, 0:T]))

            def ffn(f, base, nstat):
                n0 = FI * f

                def a_part(i, unit_end):
                    dve.wait_ge(unit_done, unit_end)
                    nc.vector.tensor_tensor(k_n(a_s, 2), halves(wk[:, 0]), bcast(rstd_b[:], 2), ALU.mult) \
                        .then_inc(a_out, 1)

                def b_part(i, unit_end):
                    dve.wait_ge(unit_done, unit_end)
                    nc.vector.tensor_tensor(k_n(b_s, 2), halves(wk[:, 1]), bcast(rstd_b[:], 2), ALU.mult) \
                        .then_inc(b_out, 1)
                    dve.wait_ge(tanh_out, i + (n0 + 1))
                    nc.vector.scalar_tensor_tensor(out=a_s, in0=t_s, scalar=1.0, in1=a_s, op0=ALU.add,
                                                   op1=ALU.mult).then_inc(h1_out, 1)
                    dve.wait_ge(h1_out, i + (n0 + 1))
                    dve.wait_ge(b_out, i + (n0 + 1))
                    nc.vector.tensor_tensor(h_s, a_s, b_s, ALU.mult).then_inc(h_out, 1)

                def h_lo(i):
                    dve.wait_ge(hh_out, i + (n0 + 1))
                    nc.vector.tensor_tensor(hl[:].rearrange("p a t -> p (a t)"), h_s,
                                            hh[:].bitcast(F32).rearrange("p a t -> p (a t)"), ALU.subtract) \
                        .then_inc(hl_out, 1)

                lo(base + 2)
                rstd(nstat)
                a_part(0, base + 1)
                lo(base + 3)
                b_part(0, base + 2)
                h_lo(0)
                if f == 0:
                    vectors()
                with dve.Fori(1, FI) as i:
                    lo_in_loop(i, base, 1)
                    a_part(i, i * 3 + base)
                    lo_in_loop(i, base, 2)
                    b_part(i, i * 3 + (base + 1))
                    lo_in_loop(i, base, 3)
                    h_lo(i)
                lo(base + 3 * FI + 1)

            def bias_cmp(k):
                b, c0, n = k // 2, 8 * (k % 2), 8 - k % 2
                dve.wait_ge(bias_cmp_mm, k + 1)
                cols = slice(C_NEGC + b * NCMP + c0, C_NEGC + b * NCMP + c0 + n)
                nc.vector.tensor_tensor(bias_c[:, b, :, c0:c0 + n],
                                        wk[:, 2, 0:8 * n].rearrange("p (c h) -> p h c", h=NHA),
                                        bcast(cst[:, cols], NHA), ALU.add).then_inc(bias_cmp_out, 1)

            def vectors():
                dve.wait_ge(vec_turned, 1)
                nc.vector.tensor_copy(vec[:, DC:V_ROWS], wk[:, 2, P + DC:P + V_ROWS]).then_inc(vec_ready, 1)
                nc.vector.tensor_copy(conv[:], wk[:, 2, 2 * P:2 * P + 176].rearrange("p (j f) -> p j f", j=4)) \
                    .then_inc(vec_ready, 1)
                dve.wait_ge(vec_ready, 2)
                nc.vector.tensor_tensor(vec[:, V_BOTH:V_COLS], vec[:, V_FINAL:V_FINAL + DC], vec[:, V_MIX2:V_MIX2 + DC],
                                        ALU.mult).then_inc(weigh_ready, 1)
                fg = vec[:, V_FINAL:V_FINAL + DC]
                step(nc.vector.memset(weigh[:, :, 0], 1.0 / D))
                step(nc.vector.tensor_tensor(weigh[:, :, 1], fg, fg, ALU.mult))
                nc.vector.tensor_scalar(weigh[:, :, 1], weigh[:, :, 1], 1.0 / D, None, ALU.mult) \
                    .then_inc(weigh_ready, 1)

            dve.wait_ge(gain_turned, 1)
            nc.vector.tensor_copy(vec[:, 0:DC], wk[:, 2, 0:DC]).then_inc(gain_ready, 1)
            lo(0)
            handoff(0, None, V_FFN1)
            dve.wait_ge(bias_mm, 1)
            dve.wait_ge(bias_in, 16 * 3)
            nc.vector.tensor_tensor(bias_rows, wk[0:16, 1, 0:BIASW], bias_mask, ALU.add).then_inc(bias_row, 1)
            lo(1)
            dve.wait_ge(small_in, 16)
            bias_cmp(0)
            ffn(0, U_FFN1, 0)
            handoff(1, 0.25, V_MIX)
            bias_cmp(1)

            def table_bc(c0, n):
                return bcast(table[:, c0:c0 + T], n)

            def proj(m):
                dve.wait_ge(unit_done, U_MIX + m + 1)
                src = halves(wk[:, m % 2])
                j = 2 * (m % 2)
                if m in (6, 7):
                    for tt in range(2):
                        last = nc.vector.tensor_scalar(v_t[:, tt, j * P:(j + 2) * P], src[:, tt],
                                                       rstd_t[:, tt:tt + 1], None, ALU.mult)
                    last.then_inc(proj_out, 1)
                    return
                if m in (8, 9):
                    dst = k_n(g_s[:, m - 8], 2)
                elif m in (4, 5):
                    dst = pool_u[:, j:j + 2, PAD:]
                else:
                    dst = (q_s if m < 2 else k_s)[:, j:j + 2]
                nc.vector.tensor_tensor(dst, src, bcast(rstd_b[:], 2), ALU.mult).then_inc(proj_out, 1)

            def rope(j):
                dst, h = (q_r, k_r)[j // 2], 2 * (j % 2)
                tmp = k_n(work[:, 4], 2)
                dve.wait_ge(swapped, j + 1)
                dve.wait_ge(table_in, 16)
                step(nc.vector.tensor_tensor(tmp, halves(acc[:, j]), table_bc(T_SIN, 2), ALU.mult))
                dve.wait_ge(rope_cos, j + 1)
                nc.vector.tensor_tensor(dst[:, h:h + 2], dst[:, h:h + 2], tmp, ALU.add).then_inc(rope_out, 1)
                dve.wait_ge(rope_out, j + 1)

            def pool_mean():
                dve.wait_ge(pool_win, 1)
                dve.wait_ge(table_in, 16)
                rc = table[:, T_RC:T_RC + 4 * T].rearrange("p (g t) -> p g t", g=4)
                for g, win in enumerate((win_a, win_b, win_a, win_b)):
                    last = nc.vector.tensor_tensor(pooled[:, g], win[:, g, PAD:], rc[:, g], ALU.mult)
                step(last)
                nc.vector.tensor_tensor(pooled, pooled, pool_u[:, :, PAD:], ALU.subtract).then_inc(pooled_out, 1)

            def pool_lo_part(j):
                for g in (2 * j, 2 * j + 1):
                    dve.wait_ge(pool_hi, 2 * j + 2)
                    nc.vector.scalar_tensor_tensor(out=ml[:, g], in0=acc[:, j, (g % 2) * T:(g % 2 + 1) * T],
                                                   scalar=vec[:, V_POOL + g:V_POOL + g + 1],
                                                   in1=mh[:, g].bitcast(F32), op0=ALU.mult, op1=ALU.subtract) \
                        .then_inc(pool_lo, 1)

            def decay(h):
                dve.wait_ge(st_mm, h + 1)
                nc.vector.tensor_tensor(st[:, h], acc[:, 2 + h % 2, 0:DEC],
                                        table[:, T_DEC + h * DEC:T_DEC + (h + 1) * DEC], ALU.mult) \
                    .then_inc(st_out, 1)

            for m in range(10):
                lo(U_MIX + m + 2)
                if m == 0:
                    rstd(1)
                if m == 9:
                    pool_lo_part(0)
                    pool_lo_part(1)
                proj(m)
                if 2 <= m < 6:
                    rope(m - 2)
                if m in (6, 7):
                    decay(2 * m - 12)
                    decay(2 * m - 11)
                if m == 7:
                    pool_mean()
            dve.wait_ge(hms_ready, 1)
            r = rsqrt(wk[:, 2, 0:8], 8)
            nc.vector.tensor_tensor(diag_h, bcast(ident, 8), bcast_in(r, P), ALU.mult).then_inc(hdiag_ready, 1)
            for j in range(2):
                dve.wait_ge(gate_tanh, j + 1)
                step(nc.vector.scalar_tensor_tensor(out=g_t[:, j], in0=g_t[:, j], scalar=1.0, in1=g_s[:, j],
                                                    op0=ALU.add, op1=ALU.mult))
            dve.wait_ge(hspread_ready, 1)
            for h in range(HR):
                last = nc.vector.scalar_tensor_tensor(out=b_h[:, h], in0=o_s[:, h],
                                                      scalar=vec[:, V_RET + h:V_RET + h + 1],
                                                      in1=wk[:, h // 2, (h % 2) * T:(h % 2 + 1) * T],
                                                      op0=ALU.mult, op1=ALU.mult)
            step(last)
            for j in range(2):
                pair = b_h[:, 2 * j:2 * j + 2]
                nc.vector.scalar_tensor_tensor(out=pair, in0=pair, scalar=0.5, in1=k_n(g_t[:, j], 2), op0=ALU.mult,
                                               op1=ALU.mult).then_inc(head_out, 1)
            for j in range(2):
                dve.wait_ge(head_hi, j + 1)
                nc.vector.tensor_tensor(ml[:, 4 + 2 * j:6 + 2 * j], b_h[:, 2 * j:2 * j + 2],
                                        mh[:, 4 + 2 * j:6 + 2 * j].bitcast(F32), ALU.subtract).then_inc(head_lo, 1)
            for m in range(4):
                lo(U_OUT1 + m + 2)
            handoff(2, 1.0, V_FFN2)
            bias_cmp(2)
            ffn(1, U_FFN2, 2)
            handoff(3, 0.25, V_BOTH)
            bias_cmp(3)

            def proj_2(m):
                dve.wait_ge(unit_done, U_IN2 + m + 1)
                bank = wk[:, m % 2] if m < 14 else wk[:, 19 - m]
                src = halves(bank)
                both = bcast(rstd_b[:], 2)
                if m in (2, 6, 7):
                    n = {2: K_A, 6: K_S, 7: K_W}[m]
                    nc.vector.tensor_tensor(kf[:, n], src[:, 0], rstd_b[:], ALU.mult)
                    if n == K_W:
                        dve.wait_ge(pv_mm, 6)
                    for tt in range(2):
                        last = nc.vector.tensor_scalar(v2[n % 2][:, tt], bank[:, T + tt * P:T + (tt + 1) * P],
                                                       rstd_t[:, tt:tt + 1], None, ALU.mult)
                    last.then_inc(proj2, 1)
                    return
                if m == 5:
                    dst = kf[:, K_CK:K_CV + 1]
                elif m < 2:
                    dst = qa_s[:, 2 * m:2 * m + 2]
                elif m < 5:
                    dst = qb_s[:, 2 * m - 6:2 * m - 4]
                elif m in GA:
                    dst = ga[:, 2 * (m - 8):2 * (m - 8) + 2]
                else:
                    c = 2 * GB.index(m)
                    dst = gb[:, c:c + 2]
                nc.vector.tensor_tensor(dst, src, both, ALU.mult).then_inc(proj2, 1)

            def attend(k):
                for s in range(SLOTS_A):
                    r, w = divmod(s, 6)
                    nh, h0, b = (2, 2 * w, 1) if w < 4 else (4, 4 * (w - 4), 0)
                    if slot_time(s) == k:
                        if s == 0:
                            dve.wait_ge(bias_ready, 16)
                            dve.wait_ge(sink_in, 16)
                        n = 512 // nh
                        hb = h0 + (0 if r == 0 else 8)
                        dve.wait_ge(score_mm, s + 1)
                        if s >= 2:
                            dve.wait_ge(exp_out, s - 1)
                        lg = logit[s % 2].rearrange("p (h n) -> p h n", h=nh)
                        nc.vector.scalar_tensor_tensor(out=lg, in0=acc[:, s % 2].rearrange("p (h n) -> p h n", h=nh),
                                                       scalar=HD ** -0.5, in1=bias[:, hb:hb + nh, 0:n][:, :, ::-1],
                                                       op0=ALU.mult, op1=ALU.add).then_inc(logit_out, 1)
                        dve.wait_ge(logit_out, s + 1)
                        top = mx[:, r, b, h0:h0 + nh]
                        step(nc.vector.tensor_reduce(top, lg, AX_X, ALU.max))
                        if r == 0:
                            step(nc.vector.tensor_tensor(top, top, sink[:, h0:h0 + nh], ALU.max))
                        nc.vector.tensor_scalar(nmx[:, r, b, h0:h0 + nh], top, -1.0, None, ALU.mult) \
                            .then_inc(neg_max, 1)
                for s in range(SLOTS_A):
                    r, w = divmod(s, 6)
                    if slot_time(s) + 2 == k and w in (3, 5):
                        b = 1 if w == 3 else 0
                        if r == 0 and b == 1:
                            continue
                        if r == 0:
                            sinks()
                            for bb in (1, 0):
                                dve.wait_ge(pv_mm, 4 if bb else 6)
                                take_y(0, bb)
                            continue
                        dve.wait_ge(pv_mm, s + 1)
                        take_y(r, b)

            def sinks():
                dve.wait_ge(exp_out, 6)
                for bb in range(2):
                    last = nc.vector.tensor_tensor(mx[:, 0, bb], sink[:], mx[:, 0, bb], ALU.subtract)
                last.then_inc(sink_gap, 1)
                dve.wait_ge(sink_exp, 1)
                step(nc.vector.tensor_tensor(sums[:, 0], sums[:, 0], mx[:, 0], ALU.add))

            def take_y(r, b):
                cf = coef[:, b]
                step(nc.vector.reciprocal(cf, sums[:, r, b]))
                bank = wk[:, 3 - b].rearrange("p (h d) -> p h d", d=HD)
                if r == 0:
                    nc.vector.tensor_tensor(y_a[:, b].rearrange("p (h d) -> p h d", d=HD), bank, bcast_in(cf, HD),
                                            ALU.mult).then_inc(y_taken, 1)
                    return
                g = gates[:, b].rearrange("p (h n) -> p n h", n=3)[:, r]
                step(nc.vector.tensor_tensor(cf, cf, g, ALU.mult))
                dst = y_b[:, b] if r == 1 else y_tmp
                nc.vector.tensor_tensor(dst.rearrange("p (h d) -> p h d", d=HD), bank, bcast_in(cf, HD),
                                        ALU.mult).then_inc(y_taken, 1)
                if r > 1:
                    dve.wait_ge(y_taken, 2 * r + 2 - b)
                    step(nc.vector.tensor_tensor(y_b[:, b], y_b[:, b], y_tmp, ALU.add))

            def blocks():
                dve.wait_ge(key_swapped, 2)
                dve.wait_ge(blk_zero, 1)
                for v in range(2):
                    for g in range(2):
                        for s in range(2):
                            rows = slice(HD * s, HD * (s + 1))
                            src = kf[rows, K_CK + v] if g == s else acc[rows, 0, v * T:(v + 1) * T]
                            src = bass.AP(tensor=src.tensor, offset=src.offset + s,
                                          ap=[list(src.ap[0]), [2, 16], [16, NCMP]])
                            pos = vec[rows, V_POSK + 16 * v:V_POSK + 16 * (v + 1)]
                            last = nc.vector.tensor_tensor(blk[rows, v, :, g * 16:g * 16 + NCMP], src,
                                                           bcast_in(pos, NCMP), ALU.add)
                last.then_inc(blk_ready, 1)

            def y_lo_part(n):
                dve.wait_ge(y_hi, n // 2 * 2 + 2)
                c0, b = 4 * (n // 2), n % 2
                bank = acc[:, 2 + b] if n < 2 else acc[:, b]
                nc.vector.tensor_tensor(ml[:, c0:c0 + 4, b * P:(b + 1) * P], k_n(bank, 4),
                                        mh[:, c0:c0 + 4, b * P:(b + 1) * P].bitcast(F32), ALU.subtract) \
                    .then_inc(y_lo, 1)

            for m in range(20):
                if m == 0:
                    dve.wait_ge(wg_split, 1)
                    nc.vector.tensor_tensor(wg_lo[:], wg_raw, wg_hi[:].bitcast(F32), ALU.subtract) \
                        .then_inc(wg_split, 1)
                    lo(U_IN2 + 2)
                    rstd_both()
                    nc.vector.tensor_scalar(half_r[:], rstd_t[:], 0.5, None, ALU.mult).then_inc(half_ready, 1)
                elif m - 1 not in CW:
                    proj_2(m - 1)
                if m in (1, 2):
                    for c in range(4 * m - 4, 4 * m):
                        nc.vector.scalar_tensor_tensor(out=x[:, c], in0=x[:, c],
                                                       scalar=vec[:, V_FINAL + c:V_FINAL + c + 1], in1=first_b,
                                                       op0=ALU.mult, op1=ALU.mult)
                if m == 2:
                    dve.wait_ge(gate_raw, 1)
                    step(nc.vector.tensor_scalar(gates[:], gates[:], 0.5, 0.5, ALU.mult, ALU.add))
                if m == 18:
                    dve.wait_ge(unit_done, U_IN2 + CW[3] + 1)
                    nc.vector.tensor_copy(hid_rows, wk[0:32, 0]).then_inc(hid_rows_out, 1)
                for half in range(2):
                    k = position_time(m, half)
                    if k is not None:
                        attend(k)
                    if half and m:
                        lo(U_IN2 + m + 2)
                    if (m, half) == (7, 0):
                        blocks()
                    if (m, half) == (8, 0):
                        dve.wait_ge(blk_hi, 1)
                        nc.vector.tensor_tensor(blk_hl[1], blk, blk_hl[0].bitcast(F32), ALU.subtract) \
                            .then_inc(blk_lo, 1)
                if m == 17:
                    y_lo_part(0)
                    y_lo_part(1)
                if m == 18:
                    dve.wait_ge(hid_turned, 1)
                    nc.vector.tensor_copy(hid_x, wk[:, 0, 0:P]).then_inc(hid_taken, 1)
                    dve.wait_ge(hid_taken, 1)
                    step(nc.vector.tensor_tensor(hid_z, hid_x, hid_x, ALU.mult))
                    step(nc.vector.tensor_scalar(hid_z, hid_z, 0.044715, 1.0, ALU.mult, ALU.add))
                    nc.vector.tensor_tensor(hid_z, hid_z, hid_x, ALU.mult).then_inc(hid_z_ready, 1)
                    dve.wait_ge(hid_tanh, 1)
                    step(nc.vector.scalar_tensor_tensor(out=hid_t, in0=hid_t, scalar=1.0, in1=hid_x, op0=ALU.add,
                                                        op1=ALU.mult))
                    nc.vector.tensor_scalar(hid_k, hid_t[:, 0:64].rearrange("p (n m) -> p n m", n=2), 0.5, None,
                                            ALU.mult)
                    for n in range(2):
                        hv = hid_t[:, 64 + 32 * n:96 + 32 * n].rearrange("p (g c) -> p g c", g=2)
                        for g in range(2):
                            last = nc.vector.tensor_scalar(
                                hv_rep[:, n, g * 64:(g + 1) * 64].rearrange("p (r c) -> p r c", r=4),
                                bcast(hv[:, g], 4), 0.5, None, ALU.mult)
                    last.then_inc(hid_ready, 1)
                if m == 19:
                    dve.wait_ge(cmp_mm, 1)
                    nc.vector.tensor_tensor(v_blk, bcast(acc[:, 1, 0:HD], 8),
                                            bcast_in(cst[:, C_BLK:C_BLK + 8], HD), ALU.mult).then_inc(vblk_ready, 1)
                    proj_2(19)
                    dve.wait_ge(cscore_mm, 1)
                    dve.wait_ge(kz_zero, 4)
                    for b in range(2):
                        lg = prob_c[:, 8 * b:8 * b + 8, 0:NCMP]
                        src = acc[:, 2, b * P:(b + 1) * P].rearrange("p (h c) -> p h c", c=16)[:, :, 0:NCMP]
                        last = nc.vector.scalar_tensor_tensor(out=lg, in0=src, scalar=HD ** -0.5, in1=bias_c[:, b],
                                                              op0=ALU.mult, op1=ALU.add)
                    step(last)
                    lg = prob_c[:, :, 0:NCMP]
                    step(nc.vector.tensor_reduce(mx_c[:], lg, AX_X, ALU.max))
                    nc.vector.tensor_tensor(lg, lg, bcast_in(mx_c[:], NCMP), ALU.subtract).then_inc(clogit, 1)
                    dve.wait_ge(cexp, 1)
                    step(nc.vector.tensor_reduce(sum_c[:], lg, AX_X, ALU.add))
                    for b in range(2):
                        cols = slice(C_VALC + b * NCMP, C_VALC + (b + 1) * NCMP)
                        last = nc.vector.tensor_tensor(lg[:, 8 * b:8 * b + 8], lg[:, 8 * b:8 * b + 8],
                                                       bcast(cst[:, cols], NHA), ALU.mult)
                    last.then_inc(cprob, 1)
                    step(nc.vector.reciprocal(sum_c[:], sum_c[:]))
                    for b in range(2):
                        g = gates[:, b].rearrange("p (h n) -> p n h", n=3)[:, 0]
                        last = nc.vector.tensor_tensor(sum_c[:, 8 * b:8 * b + 8], sum_c[:, 8 * b:8 * b + 8], g, ALU.mult)
                    step(last)
            lo(U_UP + 2)
            for b in range(2):
                dve.wait_ge(cout_mm, b + 1)
                step(nc.vector.tensor_tensor(y_tmp.rearrange("p (h d) -> p h d", d=HD),
                                             acc[:, 2 + b].rearrange("p (h d) -> p h d", d=HD),
                                             bcast_in(sum_c[:, 8 * b:8 * b + 8], HD), ALU.mult))
                nc.vector.tensor_tensor(y_b[:, b], y_b[:, b], y_tmp, ALU.add).then_inc(y_taken, 1)
                dve.wait_ge(y_taken, 2 * NBR + b + 1)
            lo(U_UP + 3)

            def up(m):
                dve.wait_ge(unit_done, U_UP + m + 1)
                dve.wait_ge(ga_tanh, 2 * m + 2)
                buf = (ga if m < 2 else gb)[:, 4 * (m % 2):4 * (m % 2) + 4]
                banks = wk[:, 2 * (m % 2):2 * (m % 2) + 2].rearrange("p b (h t) -> p (b h) t", t=T)
                nc.vector.scalar_tensor_tensor(out=buf, in0=buf, scalar=1.0, in1=banks, op0=ALU.add,
                                               op1=ALU.mult).then_inc(up_out, 1)
                if m >= 2:
                    dve.wait_ge(up_out, m + 1)
                    both = ga[:, 4 * (m - 2):4 * (m - 2) + 4]
                    nc.vector.tensor_tensor(both, both, buf, ALU.add).then_inc(merged, 1)

            up(0)
            y_lo_part(2)
            y_lo_part(3)
            lo(U_UP + 4)
            up(1)
            for m in (2, 3):
                up(m)
                cols = slice(4 * (m - 2), 4 * (m - 2) + 4)
                dve.wait_ge(merged_hi, m - 1)
                nc.vector.tensor_tensor(xl[:, cols], ga[:, cols], xh[:, cols].bitcast(F32), ALU.subtract) \
                    .then_inc(merged_lo, 1)
                if m == 2:
                    lo(U_UP + 5)
            for u in range(U_OUT2 + 2, U_OUT2 + 6):
                lo(u)
            handoff(4, 0.5, V_FFN3)

            def scaled(i, bank, dst, unit_end, out_sem):
                dve.wait_ge(unit_done, unit_end)
                nc.vector.tensor_tensor(k_n(dst, 2), halves(bank), bcast(rstd_b[:], 2), ALU.mult).then_inc(out_sem, 1)
                dve.wait_ge(out_sem, i + (2 * FI + 1))

            def taps(i, n, src, dst, f0):
                for back, signal, before in ((1, conv_1, conv_0), (2, conv_2, conv_1)):
                    for t in range(2):
                        f = f0 + t + i * 2
                        dve.wait_ge(before, i * 4 + (2 * n + t + 1))
                        tile, new = k_n(src, 2)[:, t], k_n(dst, 2)[:, t, back:]
                        nc.vector.scalar_tensor_tensor(out=new, in0=tile[:, 0:T - back],
                                                       scalar=conv[:, 2 - back, bass.ds(f, 1)], in1=new,
                                                       op0=ALU.mult, op1=ALU.add).then_inc(signal, 1)

            def ffn3_step(i, last):
                n0, base = 2 * FI, U_FFN3
                first = isinstance(i, int) and i == 0
                if first:
                    lo(base + 2)
                    rstd(4)
                else:
                    lo_in_loop(i, base, 1)
                scaled(i, wk[:, 0], a_s, base + 1 if first else i * 3 + base, a_out)
                if first:
                    lo(base + 3)
                else:
                    lo_in_loop(i, base, 2)
                taps(i, 0, a_s, conv_a, 22)
                scaled(i, wk[:, 1], b_s, base + 2 if first else i * 3 + (base + 1), b_out)
                dve.wait_ge(tanh_out, i + (n0 + 1))
                nc.vector.scalar_tensor_tensor(out=conv_a, in0=t3_s, scalar=1.0, in1=conv_a, op0=ALU.add,
                                               op1=ALU.mult).then_inc(h1_out, 1)
                taps(i, 1, b_s, conv_b, 0)
                dve.wait_ge(h1_out, i + (n0 + 1))
                dve.wait_ge(conv_2, i * 4 + 4)
                nc.vector.tensor_tensor(h3_s, conv_a, conv_b, ALU.mult).then_inc(h_out, 1)
                if not first and not last:
                    lo_in_loop(i, base, 3)
                dve.wait_ge(hh_out, i + (n0 + 1))
                nc.vector.tensor_tensor(hl[:].rearrange("p a t -> p (a t)"), h3_s,
                                        hh[:].bitcast(F32).rearrange("p a t -> p (a t)"), ALU.subtract) \
                    .then_inc(hl_out, 1)

            ffn3_step(0, False)
            with dve.Fori(1, FI - 1) as i:
                ffn3_step(i, False)
            ffn3_step(FI - 1, True)
            for c in range(DC):
                add_residual(c, 5, 0.5)
            dve.wait_ge(ms_ready, 6)
            r = rsqrt(wk[:, 3, 0:2], 2)
            nc.vector.tensor_copy(rstd_t[:], r).then_inc(rstd_ready, 1)
            dve.wait_ge(rstd_ready, 6)
            for n in (0, 2):
                half, tt = divmod(OUT_ORDER[n], 2)
                dve.wait_ge(out_turned, n + 1)
                nc.vector.tensor_scalar(out_s[:, tt, half * 512:(half + 1) * 512], out_banks[n], rstd_t[:, tt:tt + 1],
                                        None, ALU.mult).then_inc(out_copied, 1)

        @block.tensor
        def _(pe):
            def passes(dst, pairs, start, stop):
                for n, (w, v) in enumerate(pairs):
                    mm = nc.tensor.matmul(dst, w, v, start=start and n == 0, stop=stop and n == len(pairs) - 1,
                                          skip_group_check=True)
                return mm

            def col_tile(slot, t, dst, k=DC, vh=xh, vl=xl, k0=0):
                wh, wl = k_n(w_hi[:, slot], k), k_n(w_lo[:, slot], k)
                cols = slice(t * P, (t + 1) * P)
                for c in range(k):
                    mm = passes(dst, ((wh[:, c, cols], vh[:, k0 + c]), (wh[:, c, cols], vl[:, k0 + c]),
                                      (wl[:, c, cols], vh[:, k0 + c])), c == 0, c == k - 1)
                return mm

            def first_unit(slot, n):
                wh, wl = k_n(w_hi[:, slot], DC), k_n(w_lo[:, slot], DC)
                nc.tensor.matmul(wk[:, 0], zeros[:, 0:P], zeros[:], start=True, stop=False, skip_group_check=True)
                for c in range(DC):
                    pe.wait_ge(xl_ready, DC * n + c + 1)
                    for t in range(2):
                        cols = slice(t * P, (t + 1) * P)
                        mm = passes(wk[:, 0, t * T:(t + 1) * T],
                                    ((wh[:, c, cols], xh[:, c]), (wh[:, c, cols], xl[:, c]),
                                     (wl[:, c, cols], xh[:, c])), False, c == DC - 1)
                return mm

            def tok_tile(slot, tt, dst, cols):
                wh, wl = k_n(w_hi[:, slot], DC), k_n(w_lo[:, slot], DC)
                rows = slice(tt * P, (tt + 1) * P)
                for c in range(DC):
                    mm = passes(dst, ((xh[:, c, rows], wh[:, c, cols]), (xh[:, c, rows], wl[:, c, cols]),
                                      (xl[:, c, rows], wh[:, c, cols])), c == 0, c == DC - 1)
                return mm

            def open_acc():
                for b in range(4):
                    nc.tensor.matmul(acc[:, b], zeros[:, 0:P], zeros[:], start=True, stop=False,
                                     skip_group_check=True)

            def row_unit(slot, vh, vl, k0, last=False):
                wh, wl = k_n(w_hi[:, slot], 2), k_n(w_lo[:, slot], 2)
                for n in range(DC):
                    cols = slice(n * P, (n + 1) * P)
                    for c in range(2):
                        mm = passes(acc_tile(n), ((wh[:, c, cols], vh[:, k0 + c]), (wh[:, c, cols], vl[:, k0 + c]),
                                                  (wl[:, c, cols], vh[:, k0 + c])), False, last and c == 1)
                    if last:
                        mm.then_inc(acc_ready, 1)
                if last:
                    mm = nc.tensor.matmul(wk[:, 3, 2:4], zeros[:, 0:P], zeros[:, 0:2], start=True, stop=True)
                return mm

            def mean_squares(n):
                pe.wait_ge(sq_added, (DC - 1) * (SUMMED.index(n) + 1))
                for tt in range(2):
                    mm = nc.tensor.matmul(wk[:, 3, tt:tt + 1], sq[:, DC - 1, tt * P:(tt + 1) * P], mean_d[:],
                                          start=True, stop=True)
                mm.then_inc(ms_ready, 1)

            def mean_squares_both():
                pe.wait_ge(sq_ready, DC * 4)
                pe.wait_ge(weigh_ready, 2)
                for tt in range(2):
                    for c in range(DC):
                        mm = nc.tensor.matmul(wk[:, 3, 2 * tt:2 * tt + 2], sq[:, c, tt * P:(tt + 1) * P],
                                              weigh[:, c], start=c == 0, stop=c == DC - 1)
                mm.then_inc(ms_ready, 1)

            def spread(n):
                pe.wait_ge(diag_ready, 2 * (n + 1))
                for tt in range(2):
                    mm = nc.tensor.matmul(wk[:, 3, T + tt * P:T + (tt + 1) * P], ones[:], diag[:, tt],
                                          start=True, stop=True)
                mm.then_inc(spread_ready, 1)

            def ffn(f, base, n):
                n0 = FI * f
                s0, s1, s2 = base % SLOTS, (base + 1) % SLOTS, (base + 2) % SLOTS
                pe.wait_ge(lo_done, base + 1)
                first_unit(s0, n).then_inc(unit_done, 1)
                pe.wait_ge(lo_done, base + 2)
                if f == 0:
                    pe.wait_ge(bias_row, 1)
                col_tile(s1, 0, wk[:, 1, 0:T])
                mean_squares(n)
                col_tile(s1, 1, wk[:, 1, T:2 * T]).then_inc(unit_done, 1)
                if f == 0:
                    turn_vectors()
                spread(n)
                pe.wait_ge(x_ready, DC * (n + 1))
                open_acc()
                with pe.Fori(1, FI) as i:
                    pe.wait_ge(lo_done, i * 3 + base)
                    pe.wait_ge(a_out, i + n0)
                    col_tile(s2, 0, wk[:, 0, 0:T])
                    col_tile(s2, 1, wk[:, 0, T:2 * T]).then_inc(unit_done, 1)
                    pe.wait_ge(lo_done, i * 3 + (base + 1))
                    pe.wait_ge(b_out, i + n0)
                    col_tile(s0, 0, wk[:, 1, 0:T])
                    col_tile(s0, 1, wk[:, 1, T:2 * T]).then_inc(unit_done, 1)
                    pe.wait_ge(lo_done, i * 3 + (base + 2))
                    pe.wait_ge(hl_out, i + n0)
                    row_unit(s1, hh, hl, 0).then_inc(unit_done, 1)
                pe.wait_ge(lo_done, base + 3 * FI)
                pe.wait_ge(hl_out, n0 + FI)
                row_unit(s2, hh, hl, 0, last=True).then_inc(unit_done, 1)

            def turn_vectors():
                pe.wait_ge(vec_in, 16 * 10)
                pe.wait_ge(conv_in, 16 * 4)
                pe.wait_ge(bias_cmp_out, 1)
                nc.tensor.transpose(wk[:, 2, P:P + V_ROWS], vec_rows[0:V_ROWS], ident[0:V_ROWS, 0:V_ROWS])
                for j in range(4):
                    mm = nc.tensor.transpose(wk[:, 2, 2 * P + 44 * j:2 * P + 44 * (j + 1)], conv_rows[:, j],
                                             ident[0:44, 0:44])
                mm.then_inc(vec_turned, 1)

            def bias_cmp(k):
                b, c0, n = k // 2, 8 * (k % 2), 8 - k % 2
                for c in range(n):
                    y0 = OH_D0 + P * b - 16 * (c0 + c) - 31
                    mm = nc.tensor.matmul(wk[:, 2, 8 * c:8 * c + 8], oh[:, y0:y0 + P], bias_table[:, 8:16],
                                          start=True, stop=True)
                mm.then_inc(bias_cmp_mm, 1)

            pe.wait_ge(const_set, 4)
            pe.wait_ge(ident_in, 16)
            pe.wait_ge(gain_in, 16)
            nc.tensor.transpose(wk[:, 2, 0:DC], vec_rows[0:DC], ident[0:DC, 0:DC]).then_inc(gain_turned, 1)
            for c in range(DC):
                if c % 4 == 0:
                    pe.wait_ge(x_in[c // 4], 16)
                for tt in range(2):
                    mm = nc.tensor.transpose(acc_tile(c)[:, tt * P:(tt + 1) * P], x_tok[:, tt, c * P:(c + 1) * P],
                                             ident)
                mm.then_inc(acc_ready, 1)
            pe.wait_ge(bias_in, 16 * 3)
            nc.tensor.matmul(wk[0:16, 1, 0:BIASW], bias_table, oh[:, OH_D0 - BIAS_D0:OH_D0 - BIAS_D0 + BIASW],
                             start=True, stop=True).then_inc(bias_mm, 1)
            pe.wait_ge(gain_ready, 1)
            bias_cmp(0)
            ffn(0, U_FFN1, 0)
            bias_cmp(1)

            def swap_halves(j):
                src, h = (q_s, k_s)[j // 2], 2 * (j % 2)
                pe.wait_ge(proj_out, 1 + j)
                nc.tensor.matmul(acc[:, j], swap, src[:, h:h + 2], start=True, stop=True).then_inc(swapped, 1)

            def pool_mix(j):
                pe.wait_ge(pooled_out, 1)
                pe.wait_ge(pw_in, 16)
                pe.wait_ge(rope_out, j + 1)
                for g in (2 * j, 2 * j + 1):
                    mm = nc.tensor.matmul(acc[:, j, (g % 2) * T:(g % 2 + 1) * T], pool_ws[:, g], pooled[:, g],
                                          start=True, stop=True)
                mm.then_inc(pool_mm, 1)

            def scores(h):
                pe.wait_ge(rope_out, 4)
                if h >= 2:
                    pe.wait_ge(st_out, h - 1)
                bank = acc[:, 2 + h % 2]
                nc.tensor.matmul(bank[:, 0:T], k_r[:, h, 0:P], q_r[:, h], start=True, stop=True)
                nc.tensor.matmul(bank[:, T:DEC], k_r[:, h, P:T], q_r[:, h, P:T], start=True, stop=True) \
                    .then_inc(st_mm, 1)

            def head_out_mm(h):
                pe.wait_ge(st_out, h + 1)
                dst = wk[:, 2 + h // 2, (h % 2) * T:(h % 2 + 1) * T]
                nc.tensor.matmul(dst, v_t[:, 0, h * P:(h + 1) * P], st[:, h, 0:T], start=True, stop=False,
                                 skip_group_check=True)
                mm = nc.tensor.matmul(dst[:, P:T], v_t[:, 1, h * P:(h + 1) * P], st[:, h, T:DEC], start=False,
                                      stop=True, skip_group_check=True)
                if h % 2:
                    mm.then_inc(o_mm, 1)

            for m in range(10):
                u = U_MIX + m
                pe.wait_ge(lo_done, u + 1)
                if m >= 2:
                    pe.wait_ge(proj_out, m - 1)
                bank = wk[:, m % 2]
                if m == 0:
                    first_unit(u % SLOTS, 1).then_inc(unit_done, 1)
                    continue
                for half in range(2):
                    if m in (6, 7):
                        mm = tok_tile(u % SLOTS, half, bank[:, half * T:(half + 1) * T], slice(0, UC))
                    else:
                        mm = col_tile(u % SLOTS, half, bank[:, half * T:(half + 1) * T])
                    if half:
                        mm.then_inc(unit_done, 1)
                    elif m == 1:
                        mean_squares(1)
                        pe.wait_ge(x_ready, 2 * DC)
                    elif m in (6, 7):
                        scores(2 * m - 12)
                        scores(2 * m - 11)
                    elif m == 8:
                        for h in range(HR):
                            head_out_mm(h)
                    elif m == 9:
                        pe.wait_ge(osq_out, 2)
                        for h in range(HR):
                            for tt in range(2):
                                n = 2 * h + tt
                                mm = nc.tensor.matmul(wk[:, 2, n:n + 1], o_sq[:, h, tt * P:(tt + 1) * P],
                                                      mean_h[:], start=True, stop=True)
                        mm.then_inc(hms_ready, 1)
                if m == 1:
                    spread(1)
                if 1 <= m < 5:
                    swap_halves(m - 1)
                if m == 8:
                    pool_mix(0)
                    pool_mix(1)
            pe.wait_ge(pool_lo, 4)
            open_acc()
            pe.wait_ge(lo_done, U_OUT1 + 1)
            row_unit(U_OUT1 % SLOTS, mh, ml, 0).then_inc(unit_done, 1)
            pe.wait_ge(hdiag_ready, 1)
            pe.wait_ge(proj_out, 10)
            for n in range(8):
                mm = nc.tensor.matmul(wk[:, n // 4, (n % 4) * P:(n % 4 + 1) * P], ones[:], diag_h[:, n],
                                      start=True, stop=True)
            mm.then_inc(hspread_ready, 1)
            pe.wait_ge(lo_done, U_OUT1 + 2)
            row_unit((U_OUT1 + 1) % SLOTS, mh, ml, 2).then_inc(unit_done, 1)
            pe.wait_ge(head_lo, 2)
            pe.wait_ge(lo_done, U_OUT1 + 3)
            row_unit((U_OUT1 + 2) % SLOTS, mh, ml, 4).then_inc(unit_done, 1)
            pe.wait_ge(lo_done, U_OUT1 + 4)
            row_unit((U_OUT1 + 3) % SLOTS, mh, ml, 6, last=True).then_inc(unit_done, 1)
            bias_cmp(2)
            ffn(1, U_FFN2, 2)
            bias_cmp(3)

            def attend(k):
                for s in range(SLOTS_A):
                    r, w = divmod(s, 6)
                    q, z, bank = (qa_s if r == 0 else qb_s), kz[r % 2], acc[:, s % 2]
                    if slot_time(s) == k:
                        if w == 0:
                            pe.wait_ge(kz_ready, 3 if r else 1)
                            pe.wait_ge(kz_direct, 2 * r + 2)
                        if s >= 2:
                            pe.wait_ge(logit_out, s - 1)
                        if w < 4:
                            mm = nc.tensor.matmul(bank, q[:, w, P:T], z[:, w // 2], start=True, stop=True)
                        else:
                            for j in (2 * w - 8, 2 * w - 7):
                                mm = nc.tensor.matmul(bank[:, (j % 2) * T:(j % 2 + 1) * T], q[:, j, 0:P],
                                                      z[:, w - 4, :, 0:P], start=True, stop=True)
                        mm.then_inc(score_mm, 1)
                for s in range(SLOTS_A):
                    if slot_time(s) + 1 == k:
                        pe.wait_ge(exp_out, s + 1)
                        if s >= 2:
                            pe.wait_ge(prob_t_out, s - 1)
                        for n in range(4):
                            cols = slice(n * P, (n + 1) * P)
                            mm = nc.tensor.transpose(acc[:, 2 + s % 2, cols], prob[s % 2][:, cols], ident)
                        mm.then_inc(prob_turned, 1)
                for s in range(SLOTS_A):
                    if slot_time(s) + 2 == k:
                        r, w = divmod(s, 6)
                        pe.wait_ge(prob_t_out, s + 1)
                        if r and w in (0, 4):
                            pe.wait_ge(y_taken, 2 * r - (w == 0))
                        nh, h0, b = (2, 2 * w, 1) if w < 4 else (4, 4 * (w - 4), 0)
                        for h in range(nh):
                            head = h0 + h
                            dst = wk[:, 3 - b, head * HD:(head + 1) * HD]
                            g = head // 4
                            for kc in range(b + 1):
                                n = h * (b + 1) + kc
                                mm = nc.tensor.matmul(dst, prob_t[s % 2][:, n * P:(n + 1) * P],
                                                      v2[r % 2][:, kc, g * HD:(g + 1) * HD], start=kc == 0,
                                                      stop=kc == b)
                        mm.then_inc(pv_mm, 1)

            def turn_y(n):
                b = n % 2
                src, bank = ((y_a, acc[:, 2 + b]) if n < 2 else (y_b, acc[:, b]))
                for c in range(4):
                    mm = nc.tensor.transpose(bank[:, c * P:(c + 1) * P], src[:, b, c * P:(c + 1) * P], ident)
                mm.then_inc(y_turned, 1)

            for m in range(20):
                u = U_IN2 + m
                s = u % SLOTS
                pe.wait_ge(lo_done, u + 1)
                if 2 <= m < 14:
                    pe.wait_ge(proj2, m - 1)
                elif m == 14:
                    pe.wait_ge(proj2, 13)
                    pe.wait_ge(blk_lo, 1)
                    nc.tensor.matmul(wk[:, 0], zeros[:, 0:P], zeros[:], start=True, stop=False,
                                     skip_group_check=True)
                elif m == 18:
                    pe.wait_ge(proj2, 14)
                elif m == 19:
                    pe.wait_ge(hid_taken, 1)
                bank = wk[:, m % 2] if m < 14 else wk[:, 19 - m] if m >= 18 else wk[:, 0]
                for half in range(2):
                    k = position_time(m, half)
                    if k is not None:
                        attend(k)
                    if m in CW:
                        v, j0 = (m - CW[0]) // 2, 8 * (m % 2)
                        wh, wl = k_n(w_hi[:, s], 8), k_n(w_lo[:, s], 8)
                        for j in range(4 * half, 4 * half + 4):
                            bh, bl = (t[:, v, j0 + j] for t in blk_hl)
                            mm = passes(wk[0:32, 0, v * T:(v + 1) * T],
                                        ((bh, wh[:, j]), (bl, wh[:, j]), (bh, wl[:, j])), False, j0 + j == 15)
                    elif m in (2, 6, 7) and half == 1:
                        for tt in range(2):
                            mm = tok_tile(s, tt, bank[:, T + tt * P:T + (tt + 1) * P], slice(P, 2 * P))
                    elif m == 0:
                        mm = first_unit(s, 3) if half == 0 else mm
                    else:
                        mm = col_tile(s, half, bank[:, half * T:(half + 1) * T])
                    if half:
                        mm.then_inc(unit_done, 1)
                    at = (m, half)
                    if at == (0, 1):
                        mean_squares_both()
                    if at == (1, 0):
                        pe.wait_ge(x_ready, 4 * DC)
                        pe.wait_ge(wg_split, 2)
                        for tt in range(2):
                            rows = slice(tt * P, (tt + 1) * P)
                            for c in range(DC):
                                mm = passes(acc[:, 0, tt * 32:tt * 32 + 24],
                                            ((xh[:, c, rows], wg_hi[:, c]), (xh[:, c, rows], wg_lo[:, c]),
                                             (xl[:, c, rows], wg_hi[:, c])), c == 0, c == DC - 1)
                        mm.then_inc(gate_mm, 1)
                    if at == (1, 1):
                        spread(3)
                        pe.wait_ge(bias_cmp_out, 4)
                        pe.wait_ge(first_diag, 2)
                        for tt in range(2):
                            mm = nc.tensor.matmul(wk[:, 2, tt * P:(tt + 1) * P], ones[:], diag_first[:, tt],
                                                  start=True, stop=True)
                        mm.then_inc(first_spread, 1)
                    if at == (3, 0):
                        pe.wait_ge(proj2, 3)
                        pe.wait_ge(gate_raw, 1)
                        nc.tensor.matmul(acc[:, 0, 0:T], swap, kf[:, K_A], start=True, stop=True) \
                            .then_inc(key_swapped, 1)
                    if at == (6, 1):
                        pe.wait_ge(proj2, 6)
                        pe.wait_ge(logit_out, 5)
                        nc.tensor.matmul(acc[:, 0], swap, kf[:, K_CK:K_CV + 1], start=True, stop=True) \
                            .then_inc(key_swapped, 1)
                    if at == (8, 0):
                        pe.wait_ge(proj2, 8)
                        pe.wait_ge(blk_ready, 1)
                        pe.wait_ge(logit_out, 6)
                        for n in (K_S, K_W):
                            nc.tensor.matmul(acc[:, n - 1, 0:T], swap, kf[:, n], start=True, stop=True) \
                                .then_inc(key_swapped, 1)
                    if at == (16, 1):
                        pe.wait_ge(prob_t_out, SLOTS_A)
                        pe.wait_ge(y_taken, 2)
                        turn_y(0)
                        turn_y(1)
                    if at == (18, 0):
                        pe.wait_ge(hid_rows_out, 1)
                        for n in range(4):
                            mm = nc.tensor.transpose(wk[:, 0, 32 * n:32 * (n + 1)], hid_rows[:, n * P:(n + 1) * P],
                                                     ident[0:32, 0:32])
                        mm.then_inc(hid_turned, 1)
                    if at == (19, 0):
                        pe.wait_ge(hid_ready, 1)
                        pe.wait_ge(cw2_in, 16 * 3)
                        pe.wait_ge(logit_out, SLOTS_A)
                        for n in range(2):
                            nc.tensor.matmul(acc[:, 0, 0:32], cmp_w2[:, n, 0:P], hid_k[:, n], start=n == 0,
                                             stop=n == 1)
                        for n in range(2):
                            mm = nc.tensor.matmul(acc[:, 1, 0:HD], hv_rep[:, n], cmp_w2[:, n, P:P + HD], start=n == 0,
                                                  stop=n == 1)
                        mm.then_inc(cmp_mm, 1)
                    if at == (19, 1):
                        pe.wait_ge(kcz_ready, 1)
                        pe.wait_ge(y_lo, 2)
                        for b in range(2):
                            for j in range(4):
                                g = j // 2
                                mm = nc.tensor.matmul(acc[:, 2, b * P + 32 * j:b * P + 32 * (j + 1)],
                                                      qb_s[:, j, b * P:(b + 1) * P], kcz[:, :, g * 16:(g + 1) * 16],
                                                      start=True, stop=True)
                        mm.then_inc(cscore_mm, 1)
            def up(m, tiles=range(4)):
                pe.wait_ge(lo_done, U_UP + m + 1)
                for t in tiles:
                    mm = col_tile((U_UP + m) % SLOTS, t, wk[:, 2 * (m % 2) + t // 2, (t % 2) * T:(t % 2 + 1) * T],
                                  4, mh, ml, 4 * (m // 2))
                if 3 in tiles:
                    mm.then_inc(unit_done, 1)

            pe.wait_ge(y_lo, 2)
            pe.wait_ge(proj2, 16)
            up(0)
            pe.wait_ge(cprob, 1)
            for b in range(2):
                mm = nc.tensor.transpose(acc[:, 3, b * P:(b + 1) * P],
                                         prob_c[:, 8 * b:8 * b + 8].rearrange("p h c -> p (h c)"), ident)
            mm.then_inc(cturned, 1)
            pe.wait_ge(y_taken, 2 * NBR)
            up(1, range(0, 1))
            pe.wait_ge(cprob_t, 1)
            pe.wait_ge(vblk_ready, 1)
            for b in range(2):
                nc.tensor.matmul(acc[:, 2 + b], prob_ct[:, b], v_blk, start=True, stop=True).then_inc(cout_mm, 1)
            up(1, range(1, 3))
            pe.wait_ge(y_taken, 2 * NBR + 2)
            turn_y(2)
            turn_y(3)
            up(1, range(3, 4))
            pe.wait_ge(y_lo, 4)
            pe.wait_ge(up_out, 1)
            up(2)
            pe.wait_ge(y_taken, 2 * NBR + 2)
            open_acc()
            pe.wait_ge(up_out, 2)
            up(3)
            for m in range(4):
                if m % 2 == 0:
                    pe.wait_ge(merged_lo, m // 2 + 1)
                pe.wait_ge(lo_done, U_OUT2 + m + 1)
                row_unit((U_OUT2 + m) % SLOTS, xh, xl, 2 * m, last=m == 3).then_inc(unit_done, 1)
            ffn(2, U_FFN3, 4)
            for n, bank in enumerate(out_banks):
                if n == 3:
                    pe.wait_ge(x_ready, 5 * DC + 2)
                half, tt = divmod(OUT_ORDER[n], 2)
                for c in range(4 * half, 4 * half + 4):
                    if c < 4 or tt == 0:
                        pe.wait_ge(y_ready, c + 1)
                    mm = nc.tensor.transpose(bank[:, (c % 4) * P:(c % 4 + 1) * P], y_f[:, c, tt * P:(tt + 1) * P], ident)
                mm.then_inc(out_turned, 1)
            mean_squares(5)


def constants():
    import numpy as np

    f = np.float32
    small = np.zeros((P, C_COLS), f)
    small[:, C_ID:C_ID + P] = np.eye(P)
    small[:, C_SWAP:C_SWAP + P] = np.roll(np.eye(P), 64, axis=0)
    q = np.arange(P)[:, None, None] + P * np.arange(2)[None, :, None]
    valid = (q - (16 * np.arange(NCMP) + 31)[None, None, :]) >= 0
    small[:, C_NEGC:C_NEGC + 30] = np.where(valid, 0, NEG).reshape(P, 30)
    small[:, C_VALC:C_VALC + 30] = valid.reshape(P, 30)
    small[:, C_BLK:C_BLK + 8] = (np.arange(P)[:, None] // 16) == np.arange(8)[None]
    table = np.zeros((P, T_COLS), f)
    inv = (f(1.0) / (f(10000.0) ** (np.arange(0, P, 2, dtype=f) / f(P)))).astype(f)
    ang = (np.arange(T, dtype=f)[None, :] * inv[:, None]).astype(f)
    cos, sin = np.cos(ang), np.sin(ang)
    table[:, T_COS:T_COS + T] = np.concatenate([cos, cos])
    table[:, T_SIN:T_SIN + T] = np.concatenate([-sin, sin])
    keys = np.arange(P)[:, None]
    toks = np.concatenate([np.arange(T), np.arange(P)])[None]
    for h in range(HR):
        lg = np.log1p(-(2.0 ** (-5.0 - h)))
        rel = toks - keys
        table[:, T_DEC + h * DEC:T_DEC + (h + 1) * DEC] = np.where(rel >= 0, np.exp(lg * np.maximum(rel, 0)), 0) \
            * P ** -0.5
    for g, w in enumerate(POOL_WINDOWS):
        table[:, T_RC + g * T:T_RC + (g + 1) * T] = 1.0 / np.minimum(np.arange(1, T + 1), w)
    def bucket(dist):
        dist = np.maximum(dist, 0)
        exact = NBUCKET // 2
        big = exact + (np.log(np.maximum(dist, 1).astype(f) / f(exact)) / f(np.log(128 / exact))
                       * (NBUCKET - exact)).astype(np.int32)
        return np.where(dist < exact, dist, np.minimum(big, NBUCKET - 1))

    dist = np.arange(BIASW) - BIAS_D0
    onehot = (bucket(np.arange(OH_COLS) - OH_D0)[None] == np.arange(NBUCKET)[:, None]).astype(f)
    mask = np.zeros((16, BIASW), f)
    mask[:, dist < 0] = NEG
    mask[0:8, dist >= 128] = NEG
    return {"c_small": small, "c_table": table, "c_onehot": onehot, "c_mask": mask}


def kernel(**inputs):
    import numpy as _np
    import concourse.bacc as _bacc
    from concourse.bass_utils import run_bass_kernel_spmd as _run

    nc = _bacc.Bacc("TRN2", target_bir_lowering=False, num_devices=1)
    arrays, args = {}, {}
    for name, value in {**inputs, **constants()}.items():
        v = _np.ascontiguousarray(value)
        arrays[f"in_{name}"] = v
        args[name] = nc.dram_tensor(f"in_{name}", v.shape, mybir.dt.from_np(v.dtype), kind="ExternalInput").ap()
    out = nc.dram_tensor("out_0", (1, T, D), F32, kind="ExternalOutput").ap()
    build(nc, args, out)
    r = _run(nc, [arrays], core_ids=[0])
    return r.results[0]["out_0"]
```
